# Optimizing a Trainium2 kernel written in Bass

```python
import math
import jax, jax.numpy as jnp
from jax import lax
import numpy as np
import jax
import jax.numpy as jnp

D_MODEL = 1024
BATCH = 1
SEQ = 1024
DEPTH = 2

GRID_W = 64
CHUNK = 128
Q_BLOCK = 128
D_A = D_MODEL // 2
H_A = 8
HD_A = D_A // H_A
D_B = D_MODEL // 2
HEAD_DIM = 64
H_B = D_B // HEAD_DIM
KV_HEADS = 2
Q_PER_KV = H_B // KV_HEADS
D_KV = KV_HEADS * HEAD_DIM
ROPE_AXIS_DIM = HEAD_DIM // 2
ROPE_THETA = 10000.0
EPS = 1e-6
SPLITS = (D_A, D_A, D_A, D_B, D_KV, D_KV, D_B)
D_IN = sum(SPLITS)
D_MIX = D_A + D_B


def rmsnorm(x, g):
    xf = x.astype(jnp.float32)
    y = xf * lax.rsqrt(jnp.mean(xf * xf, axis=-1, keepdims=True) + EPS)
    return (y * g.astype(jnp.float32)).astype(x.dtype)

def layernorm(x, g, b):
    xf = x.astype(jnp.float32)
    mu = jnp.mean(xf, axis=-1, keepdims=True)
    var = jnp.mean(jnp.square(xf - mu), axis=-1, keepdims=True)
    y = (xf - mu) * lax.rsqrt(var + EPS)
    return (y * g.astype(jnp.float32) + b.astype(jnp.float32)).astype(x.dtype)

def axial_rope_tables(seq_len):
    rows = seq_len // GRID_W
    row = jnp.broadcast_to(jnp.arange(rows, dtype=jnp.float32)[:, None], (rows, GRID_W)).reshape(-1)
    col = jnp.broadcast_to(jnp.arange(GRID_W, dtype=jnp.float32)[None, :], (rows, GRID_W)).reshape(-1)
    inv = ROPE_THETA ** (-jnp.arange(0, ROPE_AXIS_DIM, 2, dtype=jnp.float32) / ROPE_AXIS_DIM)
    ang_r = row[:, None] * inv[None, :]
    ang_c = col[:, None] * inv[None, :]
    return jnp.cos(ang_r), jnp.sin(ang_r), jnp.cos(ang_c), jnp.sin(ang_c)

def _rot_half(x, cos, sin):
    n = x.shape[-1] // 2
    c = cos[:, None, :].astype(x.dtype)
    s = sin[:, None, :].astype(x.dtype)
    x1, x2 = x[..., :n], x[..., n:]
    return jnp.concatenate([x1 * c - x2 * s, x2 * c + x1 * s], axis=-1)

def apply_axial_rope(x, tables):
    cr, sr, cc, sc = tables
    xr = _rot_half(x[..., :ROPE_AXIS_DIM], cr, sr)
    xc = _rot_half(x[..., ROPE_AXIS_DIM:], cc, sc)
    return jnp.concatenate([xr, xc], axis=-1)

def gmlp_group(u, v, ln_g, ln_b, ws, sb):
    b, s, _ = v.shape
    nc = s // CHUNK
    vn = layernorm(v, ln_g, ln_b).reshape(b, nc, CHUNK, H_A, HD_A)
    z = jnp.einsum('hij,bcjhd->bcihd', ws, vn) + sb.T[None, None, :, :, None]
    return u * z.reshape(b, s, D_A)

def gqa_axial_attention(q, k, v, qn_g, kn_g, tables):
    b, s, _ = q.shape
    q = rmsnorm(q.reshape(b, s, H_B, HEAD_DIM), qn_g)
    k = rmsnorm(k.reshape(b, s, KV_HEADS, HEAD_DIM), kn_g)
    v = v.reshape(b, s, KV_HEADS, HEAD_DIM)
    q = apply_axial_rope(q, tables)
    k = apply_axial_rope(k, tables)
    scale = HEAD_DIM ** -0.5
    nb = s // Q_BLOCK
    qb = q.reshape(b, nb, Q_BLOCK, KV_HEADS, Q_PER_KV, HEAD_DIM).transpose(1, 0, 2, 3, 4, 5)

    def attend(qblk):
        sc = jnp.einsum('bqkgd,bskd->bkgqs', qblk, k).astype(jnp.float32) * scale
        p = jax.nn.softmax(sc, axis=-1).astype(v.dtype)
        return jnp.einsum('bkgqs,bskd->bqkgd', p, v)

    o = lax.map(attend, qb)
    return o.transpose(1, 0, 2, 3, 4, 5).reshape(b, s, D_B)

def first_inputs(seed: int = 0) -> dict:
    key = jax.random.key(seed)
    ks = jax.random.split(key, 12)
    f32 = jnp.float32
    x = jax.random.normal(ks[0], (BATCH, SEQ, D_MODEL), f32)
    w_in = jax.random.normal(ks[1], (DEPTH, D_MODEL, D_IN), f32) * D_MODEL ** -0.5
    w_out = jax.random.normal(ks[2], (DEPTH, D_MIX, D_MODEL), f32) * D_MIX ** -0.5
    pre_g = 1.0 + 0.05 * jax.random.normal(ks[3], (DEPTH, D_MODEL), f32)
    post_g = 1.0 + 0.05 * jax.random.normal(ks[4], (DEPTH, D_MODEL), f32)
    ln_a_g = 1.0 + 0.05 * jax.random.normal(ks[5], (DEPTH, D_A), f32)
    ln_a_b = 0.02 * jax.random.normal(ks[6], (DEPTH, D_A), f32)
    spatial_w = jax.random.normal(ks[7], (DEPTH, H_A, CHUNK, CHUNK), f32) * CHUNK ** -0.5
    spatial_b = 1.0 + 0.05 * jax.random.normal(ks[8], (DEPTH, H_A, CHUNK), f32)
    q_norm_g = 1.0 + 0.05 * jax.random.normal(ks[9], (DEPTH, HEAD_DIM), f32)
    k_norm_g = 1.0 + 0.05 * jax.random.normal(ks[10], (DEPTH, HEAD_DIM), f32)
    return {"x": x, "w_in": w_in, "w_out": w_out, "pre_g": pre_g, "post_g": post_g,
            "ln_a_g": ln_a_g, "ln_a_b": ln_a_b, "spatial_w": spatial_w, "spatial_b": spatial_b,
            "q_norm_g": q_norm_g, "k_norm_g": k_norm_g}

def first_block(x, w_in, w_out, pre_g, post_g, ln_a_g, ln_a_b, spatial_w, spatial_b, q_norm_g, k_norm_g):
    seq_len = x.shape[1]
    tables = axial_rope_tables(seq_len)
    idx = list(np.cumsum(SPLITS)[:-1])
    for l in range(DEPTH):
        h = rmsnorm(x, pre_g[l])
        proj = jnp.einsum('bsd,de->bse', h, w_in[l])
        u_a, v_a, g_a, q, k, v, g_b = jnp.split(proj, idx, axis=-1)
        y_a = gmlp_group(u_a, v_a, ln_a_g[l], ln_a_b[l], spatial_w[l], spatial_b[l]) * jax.nn.silu(g_a)
        y_b = gqa_axial_attention(q, k, v, q_norm_g[l], k_norm_g[l], tables) * jax.nn.silu(g_b)
        y = jnp.concatenate([y_a, y_b], axis=-1)
        out = jnp.einsum('bse,ed->bsd', y, w_out[l])
        x = x + rmsnorm(out, post_g[l])
    return x


DEPTH_2 = 1

N_MIXERS = 4
NORM_EPS = 1e-6
GLA_HEADS = 4
GLA_DK = D_MODEL // 2
GLA_DV = D_MODEL
GLA_RANK = 16
GLA_TAU = 16.0
GLA_CHUNK = 64
GLA_IN = 2 * GLA_DK + 2 * GLA_DV + GLA_RANK
RWKV_HEAD = 64
RWKV_HEADS = D_MODEL // RWKV_HEAD
RWKV_DECAY_RANK = 64
RWKV_A_RANK = 64
RWKV_GATE_RANK = 128
RWKV_GN_EPS = 64e-5
RWKV_SHIFT_MIXES = 6
SB_HEADS = 16
SB_HEAD_DIM = D_MODEL // SB_HEADS
SB_BLOCK = 128
ML_HEADS = 4
ML_DK = D_MODEL // 2
ML_DV = D_MODEL
ML_CHUNK = 64
ML_IN = 2 * ML_DK + 2 * ML_DV + 2 * ML_HEADS
FFN_DIM = 2816
CONV_WIDTH = 3


def rms_norm(x, g, eps=NORM_EPS):
    xf = x.astype(jnp.float32)
    y = xf * lax.rsqrt(jnp.mean(xf * xf, axis=-1, keepdims=True) + eps)
    return (y * g.astype(jnp.float32)).astype(x.dtype)

def _to_chunks(t, chunk):
    b, s, h, d = t.shape
    return t.reshape(b, s // chunk, chunk, h, d).transpose(1, 0, 3, 2, 4)

def _from_chunks(t):
    n, b, h, c, d = t.shape
    return t.transpose(1, 0, 3, 2, 4).reshape(b, n * c, h, d)

def _gates_to_chunks(t, chunk):
    b, s, h = t.shape
    return t.reshape(b, s // chunk, chunk, h).transpose(1, 0, 3, 2)

def gla_mixer(x, w_in, w_alpha_up, b_alpha, out_norm, w_out):
    f32 = jnp.float32
    b, s, _ = x.shape
    h, dk, dv, c = GLA_HEADS, GLA_DK // GLA_HEADS, GLA_DV // GLA_HEADS, GLA_CHUNK
    proj = x @ w_in
    q, k, v, r, a_low = jnp.split(
        proj, [GLA_DK, 2 * GLA_DK, 2 * GLA_DK + GLA_DV, 2 * GLA_DK + 2 * GLA_DV], axis=-1)
    log_alpha = jax.nn.log_sigmoid((a_low @ w_alpha_up + b_alpha).astype(f32)) / GLA_TAU
    q = q.astype(f32).reshape(b, s, h, dk) * dk ** -0.5
    k = k.astype(f32).reshape(b, s, h, dk)
    v = v.astype(f32).reshape(b, s, h, dv)
    qc, kc, vc = _to_chunks(q, c), _to_chunks(k, c), _to_chunks(v, c)
    cum = jnp.cumsum(_to_chunks(log_alpha.reshape(b, s, h, dk), c), axis=3)
    causal = jnp.tril(jnp.ones((c, c), dtype=bool))

    def step(state, inp):
        qi, ki, vi, bi = inp
        q_dec = qi * jnp.exp(bi)
        k_inv = ki * jnp.exp(-bi)
        scores = jnp.where(causal, jnp.einsum('bhtd,bhsd->bhts', q_dec, k_inv), 0.0)
        o = (jnp.einsum('bhts,bhsv->bhtv', scores, vi)
             + jnp.einsum('bhtd,bhdv->bhtv', q_dec, state))
        b_last = bi[:, :, -1:, :]
        k_end = ki * jnp.exp(b_last - bi)
        state = (state * jnp.exp(b_last)[:, :, 0, :, None]
                 + jnp.einsum('bhsd,bhsv->bhdv', k_end, vi))
        return state, o

    state0 = jnp.zeros((b, h, dk, dv), f32)
    _, o = lax.scan(step, state0, (qc, kc, vc, cum))
    o = _from_chunks(o)
    o = rms_norm(o, out_norm.reshape(h, dv)).reshape(b, s, GLA_DV)
    return (o.astype(x.dtype) * jax.nn.silu(r)) @ w_out

def rwkv7_mixer(x, mu, w_rkv, w0, w1, w2, a0, a1, a2, g1, g2, k_k, k_a, r_k, gn_g, gn_b, w_out):
    f32 = jnp.float32
    b, s, d = x.shape
    h, n = RWKV_HEADS, RWKV_HEAD
    x_prev = jnp.pad(x, ((0, 0), (1, 0), (0, 0)))[:, :-1]
    xx = x_prev - x
    xr, xw, xk, xv, xa, xg = (x + xx * mu[j] for j in range(RWKV_SHIFT_MIXES))
    r = xr @ w_rkv[0]
    k = xk @ w_rkv[1]
    v = xv @ w_rkv[2]
    w_log = -jax.nn.softplus(-(w0 + jnp.tanh(xw @ w1) @ w2).astype(f32)) - 0.5
    decay = jnp.exp(-jnp.exp(w_log))
    a = jax.nn.sigmoid((a0 + (xa @ a1) @ a2).astype(f32))
    g = jax.nn.sigmoid(xg @ g1) @ g2
    kk = (k * k_k).astype(f32).reshape(b, s, h, n)
    kk = kk / jnp.maximum(jnp.sqrt(jnp.sum(kk * kk, axis=-1, keepdims=True)), 1e-12)
    k = k.astype(f32) * (1.0 + (a - 1.0) * k_a.astype(f32))
    r = r.astype(f32).reshape(b, s, h, n)
    k = k.reshape(b, s, h, n)
    v = v.astype(f32).reshape(b, s, h, n)
    a = a.reshape(b, s, h, n)
    decay = decay.reshape(b, s, h, n)

    def step(state, inp):
        r_t, w_t, k_t, v_t, kk_t, a_t = inp
        sa = jnp.einsum('bhvk,bhk->bhv', state, -kk_t)
        state = (state * w_t[:, :, None, :]
                 + sa[..., None] * (kk_t * a_t)[:, :, None, :]
                 + v_t[..., None] * k_t[:, :, None, :])
        return state, jnp.einsum('bhvk,bhk->bhv', state, r_t)

    tm = lambda t: jnp.moveaxis(t, 1, 0)
    state0 = jnp.zeros((b, h, n, n), f32)
    _, y = lax.scan(step, state0, (tm(r), tm(decay), tm(k), tm(v), tm(kk), tm(a)))
    y = jnp.moveaxis(y, 0, 1)
    mean = jnp.mean(y, axis=-1, keepdims=True)
    var = jnp.mean(jnp.square(y - mean), axis=-1, keepdims=True)
    yn = ((y - mean) * lax.rsqrt(var + RWKV_GN_EPS)).reshape(b, s, d) * gn_g.astype(f32) + gn_b.astype(f32)
    bonus = jnp.sum(r * k * r_k.astype(f32).reshape(h, n), axis=-1, keepdims=True) * v
    out = (yn + bonus.reshape(b, s, d)).astype(x.dtype) * g
    return out @ w_out

def stick_breaking_mixer(x, w_qkv, w_out):
    f32 = jnp.float32
    b, s, d = x.shape
    h, dh, qb_len = SB_HEADS, SB_HEAD_DIM, SB_BLOCK
    q, k, v = jnp.split(x @ w_qkv, 3, axis=-1)
    q = q.reshape(b, s, h, dh) * dh ** -0.5
    k = k.reshape(b, s, h, dh)
    v = v.reshape(b, s, h, dh)
    n_blocks = s // qb_len
    q_blocks = q.reshape(b, n_blocks, qb_len, h, dh).transpose(1, 0, 3, 2, 4)
    starts = jnp.arange(n_blocks, dtype=jnp.int32) * qb_len
    key_pos = jnp.arange(s, dtype=jnp.int32)

    def block(args):
        q_blk, start = args
        z = jnp.einsum('bhqd,bkhd->bhqk', q_blk, k).astype(f32)
        q_pos = start + jnp.arange(qb_len, dtype=jnp.int32)
        before = key_pos[None, :] < q_pos[:, None]
        log_keep = jnp.where(before, jax.nn.log_sigmoid(-z), 0.0)
        suffix = lax.cumsum(log_keep, axis=3, reverse=True)
        log_w = jax.nn.log_sigmoid(z) + suffix - log_keep
        w = jnp.where(before, jnp.exp(log_w), 0.0)
        return jnp.einsum('bhqk,bkhd->bhqd', w.astype(v.dtype), v)

    o = lax.map(block, (q_blocks, starts))
    o = o.transpose(1, 0, 3, 2, 4).reshape(b, s, d)
    return o @ w_out

def mlstm_mixer(x, w_in, b_if, out_norm, w_out):
    f32 = jnp.float32
    b, s, _ = x.shape
    h, dk, dv, c = ML_HEADS, ML_DK // ML_HEADS, ML_DV // ML_HEADS, ML_CHUNK
    proj = x @ w_in
    q, k, v, o_pre, if_pre = jnp.split(
        proj, [ML_DK, 2 * ML_DK, 2 * ML_DK + ML_DV, 2 * ML_DK + 2 * ML_DV], axis=-1)
    if_pre = (if_pre + b_if).astype(f32)
    i_pre = if_pre[..., :h]
    log_f = jax.nn.log_sigmoid(if_pre[..., h:])
    qc = _to_chunks(q.astype(f32).reshape(b, s, h, dk), c)
    kc = _to_chunks(k.astype(f32).reshape(b, s, h, dk) * dk ** -0.5, c)
    vc = _to_chunks(v.astype(f32).reshape(b, s, h, dv), c)
    ic = _gates_to_chunks(i_pre, c)
    cum_f = jnp.cumsum(_gates_to_chunks(log_f, c), axis=-1)
    causal = jnp.tril(jnp.ones((c, c), dtype=bool))

    def step(carry, inp):
        c_st, n_st, m_prev = carry
        qi, ki, vi, ii, bi = inp
        d_log = jnp.where(causal, bi[..., :, None] - bi[..., None, :] + ii[..., None, :], -jnp.inf)
        inter = bi + m_prev[..., None]
        m_t = jnp.maximum(inter, jnp.max(d_log, axis=-1))
        w_intra = jnp.exp(d_log - m_t[..., None])
        scale = jnp.exp(inter - m_t)
        qk = jnp.einsum('bhtd,bhsd->bhts', qi, ki) * w_intra
        num = (jnp.einsum('bhts,bhsv->bhtv', qk, vi)
               + scale[..., None] * jnp.einsum('bhtd,bhdv->bhtv', qi, c_st))
        den = jnp.sum(qk, axis=-1) + scale * jnp.einsum('bhtd,bhd->bht', qi, n_st)
        h_out = num / jnp.maximum(jnp.abs(den), jnp.exp(-m_t))[..., None]
        b_last = bi[..., -1]
        g_end = b_last[..., None] - bi + ii
        m_new = jnp.maximum(b_last + m_prev, jnp.max(g_end, axis=-1))
        w_end = jnp.exp(g_end - m_new[..., None])
        carry_scale = jnp.exp(b_last + m_prev - m_new)
        c_st = carry_scale[..., None, None] * c_st + jnp.einsum('bhs,bhsd,bhsv->bhdv', w_end, ki, vi)
        n_st = carry_scale[..., None] * n_st + jnp.einsum('bhs,bhsd->bhd', w_end, ki)
        return (c_st, n_st, m_new), h_out

    carry0 = (jnp.zeros((b, h, dk, dv), f32), jnp.zeros((b, h, dk), f32), jnp.zeros((b, h), f32))
    _, hs = lax.scan(step, carry0, (qc, kc, vc, ic, cum_f))
    hs = _from_chunks(hs)
    hs = rms_norm(hs, out_norm.reshape(h, dv)).reshape(b, s, ML_DV)
    return (hs.astype(x.dtype) * jax.nn.sigmoid(o_pre)) @ w_out

def conv_ffn(x, w_up, conv_w, conv_b, w_down):
    s = x.shape[1]
    u = x @ w_up
    u_pad = jnp.pad(u, ((0, 0), (CONV_WIDTH - 1, 0), (0, 0)))
    u = sum(u_pad[:, j:j + s] * conv_w[j] for j in range(CONV_WIDTH)) + conv_b
    gate, up = jnp.split(u, 2, axis=-1)
    return (jax.nn.silu(gate) * up) @ w_down

def second_inputs(seed: int = 0) -> dict:
    key = jax.random.key(seed)
    ks = iter(jax.random.split(key, 96))
    f32 = jnp.float32
    D, F2 = D_MODEL, 2 * FFN_DIM

    def nrm(shape, scale):
        return scale * jax.random.normal(next(ks), shape, f32)

    def dense(fan_in, shape):
        return nrm(shape, fan_in ** -0.5)

    def gain(n):
        return 1.0 + nrm((n,), 0.02)

    def unif(shape, lo, hi):
        return jax.random.uniform(next(ks), shape, f32, lo, hi)

    p = {}

    def ffn_params(i):
        p[f"l{i}_norm2"] = gain(D)
        p[f"l{i}_ffn_w_up"] = dense(D, (D, F2))
        p[f"l{i}_ffn_conv_w"] = dense(CONV_WIDTH, (CONV_WIDTH, F2))
        p[f"l{i}_ffn_conv_b"] = nrm((F2,), 0.02)
        p[f"l{i}_ffn_w_down"] = dense(FFN_DIM, (FFN_DIM, D))

    p["x"] = nrm((BATCH, SEQ, D), 1.0)
    p["l0_norm1"] = gain(D)
    p["l0_gla_w_in"] = dense(D, (D, GLA_IN))
    p["l0_gla_w_alpha_up"] = dense(GLA_RANK, (GLA_RANK, GLA_DK))
    p["l0_gla_b_alpha"] = nrm((GLA_DK,), 0.1)
    p["l0_gla_out_norm"] = gain(GLA_DV)
    p["l0_gla_w_out"] = dense(GLA_DV, (GLA_DV, D))
    ffn_params(0)
    p["l1_norm1"] = gain(D)
    p["l1_rwkv_mu"] = unif((RWKV_SHIFT_MIXES, D), 0.0, 1.0)
    p["l1_rwkv_w_rkv"] = dense(D, (3, D, D))
    p["l1_rwkv_w0"] = unif((D,), -6.0, -1.0)
    p["l1_rwkv_w1"] = dense(D, (D, RWKV_DECAY_RANK))
    p["l1_rwkv_w2"] = nrm((RWKV_DECAY_RANK, D), 0.1 * RWKV_DECAY_RANK ** -0.5)
    p["l1_rwkv_a0"] = nrm((D,), 0.1)
    p["l1_rwkv_a1"] = dense(D, (D, RWKV_A_RANK))
    p["l1_rwkv_a2"] = dense(RWKV_A_RANK, (RWKV_A_RANK, D))
    p["l1_rwkv_g1"] = dense(D, (D, RWKV_GATE_RANK))
    p["l1_rwkv_g2"] = dense(RWKV_GATE_RANK, (RWKV_GATE_RANK, D))
    p["l1_rwkv_k_k"] = 0.85 + nrm((D,), 0.05)
    p["l1_rwkv_k_a"] = 1.0 + nrm((D,), 0.05)
    p["l1_rwkv_r_k"] = nrm((D,), 0.1)
    p["l1_rwkv_gn_g"] = gain(D)
    p["l1_rwkv_gn_b"] = nrm((D,), 0.02)
    p["l1_rwkv_w_out"] = dense(D, (D, D))
    ffn_params(1)
    p["l2_norm1"] = gain(D)
    p["l2_sb_w_qkv"] = dense(D, (D, 3 * D))
    p["l2_sb_w_out"] = dense(D, (D, D))
    ffn_params(2)
    p["l3_norm1"] = gain(D)
    p["l3_ml_w_in"] = dense(D, (D, ML_IN))
    p["l3_ml_b_if"] = jnp.concatenate([nrm((ML_HEADS,), 0.1), unif((ML_HEADS,), 3.0, 6.0)])
    p["l3_ml_out_norm"] = gain(ML_DV)
    p["l3_ml_w_out"] = dense(ML_DV, (ML_DV, D))
    ffn_params(3)
    p["final_norm"] = gain(D)
    return p

def second_block(x,
              l0_norm1, l0_gla_w_in, l0_gla_w_alpha_up, l0_gla_b_alpha, l0_gla_out_norm, l0_gla_w_out,
              l0_norm2, l0_ffn_w_up, l0_ffn_conv_w, l0_ffn_conv_b, l0_ffn_w_down,
              l1_norm1, l1_rwkv_mu, l1_rwkv_w_rkv, l1_rwkv_w0, l1_rwkv_w1, l1_rwkv_w2,
              l1_rwkv_a0, l1_rwkv_a1, l1_rwkv_a2, l1_rwkv_g1, l1_rwkv_g2,
              l1_rwkv_k_k, l1_rwkv_k_a, l1_rwkv_r_k, l1_rwkv_gn_g, l1_rwkv_gn_b, l1_rwkv_w_out,
              l1_norm2, l1_ffn_w_up, l1_ffn_conv_w, l1_ffn_conv_b, l1_ffn_w_down,
              l2_norm1, l2_sb_w_qkv, l2_sb_w_out,
              l2_norm2, l2_ffn_w_up, l2_ffn_conv_w, l2_ffn_conv_b, l2_ffn_w_down,
              l3_norm1, l3_ml_w_in, l3_ml_b_if, l3_ml_out_norm, l3_ml_w_out,
              l3_norm2, l3_ffn_w_up, l3_ffn_conv_w, l3_ffn_conv_b, l3_ffn_w_down,
              final_norm):
    mixers = (
        lambda h: gla_mixer(h, l0_gla_w_in, l0_gla_w_alpha_up, l0_gla_b_alpha, l0_gla_out_norm, l0_gla_w_out),
        lambda h: rwkv7_mixer(h, l1_rwkv_mu, l1_rwkv_w_rkv, l1_rwkv_w0, l1_rwkv_w1, l1_rwkv_w2,
                              l1_rwkv_a0, l1_rwkv_a1, l1_rwkv_a2, l1_rwkv_g1, l1_rwkv_g2,
                              l1_rwkv_k_k, l1_rwkv_k_a, l1_rwkv_r_k, l1_rwkv_gn_g, l1_rwkv_gn_b,
                              l1_rwkv_w_out),
        lambda h: stick_breaking_mixer(h, l2_sb_w_qkv, l2_sb_w_out),
        lambda h: mlstm_mixer(h, l3_ml_w_in, l3_ml_b_if, l3_ml_out_norm, l3_ml_w_out),
    )
    norm1 = (l0_norm1, l1_norm1, l2_norm1, l3_norm1)
    norm2 = (l0_norm2, l1_norm2, l2_norm2, l3_norm2)
    ffns = (
        (l0_ffn_w_up, l0_ffn_conv_w, l0_ffn_conv_b, l0_ffn_w_down),
        (l1_ffn_w_up, l1_ffn_conv_w, l1_ffn_conv_b, l1_ffn_w_down),
        (l2_ffn_w_up, l2_ffn_conv_w, l2_ffn_conv_b, l2_ffn_w_down),
        (l3_ffn_w_up, l3_ffn_conv_w, l3_ffn_conv_b, l3_ffn_w_down),
    )
    for layer in range(DEPTH_2):
        x = x + mixers[layer % N_MIXERS](rms_norm(x, norm1[layer]))
        x = x + conv_ffn(rms_norm(x, norm2[layer]), *ffns[layer])
    return rms_norm(x, final_norm)


def setup_inputs(seed=0):
    out = dict(first_inputs(seed))
    for name, value in second_inputs(seed + 1).items():
        if name != "x":
            out[name + "_2"] = value
    return out


def reference(
    x, w_in, w_out, pre_g, post_g, ln_a_g, ln_a_b, spatial_w, spatial_b, q_norm_g, k_norm_g,
    l0_norm1_2, l0_gla_w_in_2, l0_gla_w_alpha_up_2, l0_gla_b_alpha_2, l0_gla_out_norm_2,
    l0_gla_w_out_2, l0_norm2_2, l0_ffn_w_up_2, l0_ffn_conv_w_2, l0_ffn_conv_b_2,
    l0_ffn_w_down_2, l1_norm1_2, l1_rwkv_mu_2, l1_rwkv_w_rkv_2, l1_rwkv_w0_2, l1_rwkv_w1_2,
    l1_rwkv_w2_2, l1_rwkv_a0_2, l1_rwkv_a1_2, l1_rwkv_a2_2, l1_rwkv_g1_2, l1_rwkv_g2_2,
    l1_rwkv_k_k_2, l1_rwkv_k_a_2, l1_rwkv_r_k_2, l1_rwkv_gn_g_2, l1_rwkv_gn_b_2,
    l1_rwkv_w_out_2, l1_norm2_2, l1_ffn_w_up_2, l1_ffn_conv_w_2, l1_ffn_conv_b_2,
    l1_ffn_w_down_2, l2_norm1_2, l2_sb_w_qkv_2, l2_sb_w_out_2, l2_norm2_2, l2_ffn_w_up_2,
    l2_ffn_conv_w_2, l2_ffn_conv_b_2, l2_ffn_w_down_2, l3_norm1_2, l3_ml_w_in_2, l3_ml_b_if_2,
    l3_ml_out_norm_2, l3_ml_w_out_2, l3_norm2_2, l3_ffn_w_up_2, l3_ffn_conv_w_2,
    l3_ffn_conv_b_2, l3_ffn_w_down_2, final_norm_2,
):
    x = first_block(
        x, w_in, w_out, pre_g, post_g, ln_a_g, ln_a_b, spatial_w, spatial_b, q_norm_g, k_norm_g,
    )
    return second_block(
        x, l0_norm1_2, l0_gla_w_in_2, l0_gla_w_alpha_up_2, l0_gla_b_alpha_2, l0_gla_out_norm_2,
        l0_gla_w_out_2, l0_norm2_2, l0_ffn_w_up_2, l0_ffn_conv_w_2, l0_ffn_conv_b_2,
        l0_ffn_w_down_2, l1_norm1_2, l1_rwkv_mu_2, l1_rwkv_w_rkv_2, l1_rwkv_w0_2, l1_rwkv_w1_2,
        l1_rwkv_w2_2, l1_rwkv_a0_2, l1_rwkv_a1_2, l1_rwkv_a2_2, l1_rwkv_g1_2, l1_rwkv_g2_2,
        l1_rwkv_k_k_2, l1_rwkv_k_a_2, l1_rwkv_r_k_2, l1_rwkv_gn_g_2, l1_rwkv_gn_b_2,
        l1_rwkv_w_out_2, l1_norm2_2, l1_ffn_w_up_2, l1_ffn_conv_w_2, l1_ffn_conv_b_2,
        l1_ffn_w_down_2, l2_norm1_2, l2_sb_w_qkv_2, l2_sb_w_out_2, l2_norm2_2, l2_ffn_w_up_2,
        l2_ffn_conv_w_2, l2_ffn_conv_b_2, l2_ffn_w_down_2, l3_norm1_2, l3_ml_w_in_2,
        l3_ml_b_if_2, l3_ml_out_norm_2, l3_ml_w_out_2, l3_norm2_2, l3_ffn_w_up_2,
        l3_ffn_conv_w_2, l3_ffn_conv_b_2, l3_ffn_w_down_2, final_norm_2,
    )


_drawn_inputs = setup_inputs


def setup_inputs(seed=0):
    import zlib

    import numpy as np

    out = dict(_drawn_inputs(seed))
    spreads = {}
    factors = {'ln_a_b': 2.915,
     'q_norm_g': 8.0,
     'k_norm_g': 8.0,
     'l0_norm1_2': 3.939,
     'l0_gla_b_alpha_2': 3.648,
     'l0_gla_out_norm_2': 8.0,
     'l0_norm2_2': 6.1,
     'l0_ffn_conv_b_2': 6.28,
     'final_norm_2': 2.891}
    for name, (base, spread) in spreads.items():
        noise = np.random.default_rng([zlib.crc32(name.encode()), seed]).standard_normal(out[name].shape)
        drawn = base * np.exp(spread * noise) if base else spread * noise
        out[name] = jnp.asarray(drawn.astype(out[name].dtype))
    for name, factor in factors.items():
        out[name] = (out[name] * factor).astype(out[name].dtype)
    return out
```

```python
from contextlib import ExitStack

import concourse.bass as bass
from concourse import mybir

ALU = mybir.AluOpType
ACT = mybir.ActivationFunctionType
AX = mybir.AxisListType
F32 = mybir.dt.float32
F32R = mybir.dt.float32r
U32 = mybir.dt.uint32

P = 128
SEQ = 1024
D = 1024
TT = SEQ // P
KT = D // P
UNIT = 256
DEPTH = 2
EPS = 1e-6
D_A = 512
H_A = 8
HD = 64
H_B = 8
KV = 2
D_IN = 2816
COL_U, COL_VA, COL_GA, COL_Q, COL_KV, COL_GB = 0, 512, 1024, 1536, 2048, 2304
QKH = H_B + KV
GH = 4
DK = 128
DV = 256
RANK = 16
TAU = 16.0
CH = 64
FFN = 2816
FT = FFN // P

KB = 1024


def plane(ap):
    return ap.bitcast(F32)


class Program:

    def __init__(self, nc, ctx, consts):
        self.nc, self.ctx = nc, ctx
        self.base = nc.sbuf_base + (-nc.sbuf_base) % 64
        self.room = nc.sbuf_usable_end - self.base
        self.n = 0
        self.phase_sems = []
        self.hT_hi = self.at("hT_hi", [P, KT, SEQ], 0, F32R)
        self.hT_lo = self.at("hT_lo", [P, KT, SEQ], 32, F32R)
        self.w_raw = self.at("w_raw", [P, 2, KT * UNIT], 64)
        self.w_hi = self.at("w_hi", [P, 2, KT * UNIT], 80, F32R)
        self.w_lo = self.at("w_lo", [P, 2, KT * UNIT], 96, F32R)
        self.B = 112
        self.ident = self.at("ident", [P, P], 206)
        self.eps = self.at("eps", [P, 1], 206.5)
        self.gain = self.at("gain", [P, KT], 206.75)
        self.psum = [ctx.enter_context(nc.psum_tensor(f"bank{i}", [P, 512], F32)) for i in range(0)]
        self.ps = ctx.enter_context(nc.psum_tensor("ps", [P, 8, 512], F32))

    def at(self, name, shape, kb, dt=F32):
        size = 4
        for s in shape[1:]:
            size *= s
        off = self.base + int(kb * KB)
        assert kb * KB + size <= self.room, (name, kb, size, self.room)
        self.n += 1
        return self.nc.alloc_sbuf_tensor_at(f"{name}_{self.n}", shape, dt, offset=off)

    def sem(self, name):
        self.n += 1
        sem = self.nc.alloc_semaphore(name=f"{name}_{self.n}")
        self.phase_sems.append(sem)
        return sem

    def end_phase(self):
        self.nc.clear_and_free_semaphores(self.phase_sems)
        self.nc.all_engine_barrier()
        self.phase_sems = []


class Weights:

    def __init__(self, prog, src, done, per_unit, size=KT * UNIT, pieces=1):
        self.p, self.src, self.size, self.pieces = prog, src, size, pieces
        self.done, self.per_unit = done, per_unit
        self.landed = [prog.sem("w_landed0"), prog.sem("w_landed1")]
        self.hi_ready = prog.sem("w_hi_ready")
        self.lo_ready = prog.sem("w_lo_ready")

    def load(self, sp, u, slot=None, reused=True):
        slot = u % 2 if slot is None else slot
        if reused:
            sp.wait_ge(self.lo_ready, u - 1)
        for dst, src in self.src(u, self.p.w_raw[:, slot, 0:self.size]):
            sp.dma_start(dst, src).then_inc(self.landed[slot], 16)

    def split_hi(self, act, u, slot=None, visit=None, reused=True):
        slot, visit = (u % 2, u // 2) if slot is None else (slot, visit)
        act.wait_ge(self.landed[slot], visit * (16 * self.pieces) + 16 * self.pieces)
        if reused:
            act.wait_ge(self.done, u * self.per_unit - self.per_unit)
        self.p.nc.scalar.activation(self.p.w_hi[:, slot, 0:self.size], self.p.w_raw[:, slot, 0:self.size],
                                    ACT.Copy).then_inc(self.hi_ready, 1)

    def split_lo(self, dve, u, slot=None):
        slot = u % 2 if slot is None else slot
        dve.wait_ge(self.hi_ready, u + 1)
        self.p.nc.vector.tensor_tensor(self.p.w_lo[:, slot, 0:self.size], self.p.w_raw[:, slot, 0:self.size],
                                       plane(self.p.w_hi[:, slot, 0:self.size]),
                                       ALU.subtract).then_inc(self.lo_ready, 1)

    def first_two(self, load=None, hi=None, lo=None):
        for u in range(2):
            if load is not None:
                self.load(load, u, reused=False)
            if hi is not None:
                self.split_hi(hi, u, reused=False)
            if lo is not None:
                self.split_lo(lo, u)


def three_products(nc, out, a_hi, a_lo, b_hi, b_lo, first, last):
    nc.tensor.matmul(out, a_hi, b_hi, start=first, stop=False)
    nc.tensor.matmul(out, a_hi, b_lo, start=False, stop=False)
    return nc.tensor.matmul(out, a_lo, b_hi, start=False, stop=last)


class Turn:

    GROUPS = 2 * KT

    def __init__(self, prog, gain=True):
        self.p, self.gain = prog, gain
        self.turned = prog.sem("turned")
        self.hi_done = prog.sem("turn_hi_done")
        self.lo_done = prog.sem("turn_lo_done")

    def pe(self, pe, src, first_bank=0):
        nc = self.p.nc
        for g in range(self.GROUPS):
            k, half = g // 2, g % 2
            if g >= 4:
                pe.wait_ge(self.lo_done, g - 3)
            for j in range(4):
                mm = nc.tensor.transpose(self.p.ps[:, g % 4, j * P:(j + 1) * P], src(half * 4 + j, k),
                                         self.p.ident[:])
            mm.then_inc(self.turned, 1)

    def act(self, act):
        for g in range(self.GROUPS):
            k, half = g // 2, g % 2
            act.wait_ge(self.turned, g + 1)
            scale = self.p.gain[:, k:k + 1] if self.gain else 1.0
            self.p.nc.scalar.activation(self.p.hT_hi[:, k, half * 512:(half + 1) * 512], self.p.ps[:, g % 4, :],
                                        ACT.Copy, scale=scale).then_inc(self.hi_done, 1)

    def dve(self, dve):
        for g in range(self.GROUPS):
            k, half = g // 2, g % 2
            dve.wait_ge(self.hi_done, g + 1)
            hi = plane(self.p.hT_hi[:, k, half * 512:(half + 1) * 512])
            lo = self.p.hT_lo[:, k, half * 512:(half + 1) * 512]
            scale = self.p.gain[:, k:k + 1] if self.gain else 1.0
            self.p.nc.vector.scalar_tensor_tensor(lo, self.p.ps[:, g % 4, :], scale, hi, ALU.mult,
                                                  ALU.subtract).then_inc(self.lo_done, 1)


class RowNorm:

    def __init__(self, prog, x, junk, stat):
        self.p, self.x, self.junk, self.stat = prog, x, junk, stat
        self.squared = prog.sem("squared")
        self.mean_done = prog.sem("mean_done")
        self.rooted = prog.sem("rooted")
        self.inverted = prog.sem("inverted")
        self.scaled = prog.sem("scaled")

    def act(self, act, wait_x):
        nc = self.p.nc
        for t in range(TT):
            wait_x(act, t)
            nc.scalar.activation(self.junk[:], self.x[:, t, :], ACT.Square,
                                 accum_out=self.stat[:, t:t + 1]).then_inc(self.squared, 1)
            act.wait_ge(self.squared, t + 1)
        act.wait_ge(self.mean_done, 1)
        nc.scalar.activation(self.stat[:, 8:16], self.stat[:, 16:24], ACT.Sqrt).then_inc(self.rooted, 1)

    def dve(self, dve):
        nc = self.p.nc
        dve.wait_ge(self.squared, TT)
        nc.vector.tensor_scalar(self.stat[:, 16:24], self.stat[:, 0:8], 1.0 / D, EPS, ALU.mult,
                                ALU.add).then_inc(self.mean_done, 1)
        dve.wait_ge(self.rooted, 1)
        nc.vector.reciprocal(self.stat[:, 24:32], self.stat[:, 8:16]).then_inc(self.inverted, 1)
        dve.wait_ge(self.inverted, 1)
        for t in range(TT):
            nc.vector.tensor_scalar(self.x[:, t, :], self.x[:, t, :], self.stat[:, 24 + t:25 + t], None,
                                    ALU.mult).then_inc(self.scaled, 1)


def pe_rows_unit(prog, pe, w, unit, slot, acc_free, acc_ready, free_base, hT_hi, hT_lo):
    nc = prog.nc
    pe.wait_ge(w.lo_ready, unit + 1)
    for t in range(TT):
        if free_base is not None or t >= 4:
            pe.wait_ge(acc_free, (free_base if free_base is not None else 0) + t - 3)
        for k in range(KT):
            tok = slice(t * P, (t + 1) * P)
            col = slice(k * UNIT, (k + 1) * UNIT)
            mm = three_products(nc, prog.ps[:, t % 4, 0:UNIT], hT_hi[:, k, tok], hT_lo[:, k, tok],
                                prog.w_hi[:, slot, col], prog.w_lo[:, slot, col], k == 0, k == KT - 1)
            if k == KT - 1:
                mm.then_inc(acc_ready, 1)


def make_constants(prog):
    nc = prog.nc
    made = prog.sem("ident_made")
    with nc.Block() as block:
        @block.gpsimd
        def _(pool):
            nc.gpsimd.memset(prog.ident[:], 0.0).then_inc(made, 1)
            nc.gpsimd.memset(prog.eps[:], EPS)
            pool.wait_ge(made, 1)
            nc.gpsimd.affine_select(out=prog.ident[:], in_=prog.ident[:], compare_op=ALU.not_equal, fill=1.0,
                                    base=0, pattern=[[-1, P]], channel_multiplier=1).then_inc(made, 1)
            pool.wait_ge(made, 2)


def mixer_inputs(prog, l, x_src, a, buf):
    nc = prog.nc
    kb = prog.B
    X = prog.at("X", [P, TT, D], kb)
    QKV = prog.at("QKV", [P, TT, 768], kb)
    VA = prog.at("VA", [P, TT, D_A], kb + 24)
    U = prog.at("U", [P, TT, D_A], kb + 40)
    G = prog.at("G", [P, TT, D_A], kb + 56)
    s = kb + 72
    rope = prog.at("rope", [P, 2, TT, HD], s)
    ln_gb = prog.at("ln_gb", [P, 2, D_A], s + 4)
    qkg = prog.at("qkg", [P, 2, HD], s + 8)
    stat = prog.at("stat", [P, 64], s + 8.5)
    spb = prog.at("spb", [P, H_A], s + 8.75)
    hst = prog.at("hst", [P, 4, TT, QKH], s + 9)
    bn = prog.at("bn", [P, TT, 6], s + 10.25)
    mv = prog.at("mv", [P, TT, 2], s + 10.5)
    rstd = prog.at("rstd", [P, 2, TT], s + 10.75)
    sq = prog.at("sq", [P, QKH * HD], s + 11)
    rot = prog.at("rot", [P, QKH * HD], s + 13.5)
    junk = prog.at("junk", [P, D], kb + 32)
    wsT = prog.at("wsT", [P, H_A, P], s + 16)
    wsR = prog.at("wsR", [P, H_A, P], kb + 56)
    order = [COL_KV, COL_Q, COL_Q + UNIT, COL_VA, COL_VA + UNIT, COL_U, COL_U + UNIT,
             COL_GA, COL_GA + UNIT, COL_GB, COL_GB + UNIT]
    NU = len(order)
    wv = a["w_in"][l].rearrange("(k p) n -> p k n", p=P)

    def src(u, raw):
        return [(raw.rearrange("p (k n) -> p k n", k=KT), wv[:, :, order[u]:order[u] + UNIT])]

    acc_ready = prog.sem("acc_ready")
    w = Weights(prog, src, acc_ready, TT)
    turn = Turn(prog)
    norm = RowNorm(prog, X, junk, stat)
    x_landed = [prog.sem(f"x_landed{i}") for i in range(TT // 2)]
    small_landed = prog.sem("small_landed")
    acc_free = prog.sem("acc_free")
    ws_turned = prog.sem("ws_turned")
    ws_taken = prog.sem("ws_taken")
    head_sq = prog.sem("head_sq")
    head_sum = prog.sem("head_sum")
    head_root = prog.sem("head_root")
    head_inv = prog.sem("head_inv")
    rope_step = prog.sem("rope_step")
    ln_stat = prog.sem("ln_stat")
    ln_root = prog.sem("ln_root")
    ln_step = prog.sem("ln_step")
    ln_scaled = prog.sem("ln_scaled")
    ln_done = prog.sem("ln_done")
    ga_used = prog.sem("ga_used")
    z_ready = prog.sem("z_ready")
    ya_done = prog.sem("ya_done")

    with nc.Block() as block:
        @block.sync
        def _(sp):
            sp.dma_start(prog.gain[:], a["pre_g"][l].rearrange("(k p) -> p k", p=P),
                         allow_slow_non_contiguous=True).then_inc(small_landed, 16)
            xv = x_src.rearrange("(t p) d -> p t d", p=P)
            for t in range(0, TT, 2):
                sp.dma_start(X[:, t:t + 2, :], xv[:, t:t + 2, :]).then_inc(x_landed[t // 2], 16)
            w.first_two(load=sp)
            sp.dma_start(wsR[:], a["spatial_w"][l].rearrange("h i j -> i h j")).then_inc(small_landed, 16)
            sp.dma_start(spb[:], a["spatial_b"][l].rearrange("h i -> i h"),
                         allow_slow_non_contiguous=True).then_inc(small_landed, 16)
            sp.dma_start(rope[:], a["rope"].rearrange("c (t p) d -> p c t d", p=P)).then_inc(small_landed, 16)
            sp.dma_start(ln_gb[:, 0, :], a["ln_a_g"][l:l + 1, :].to_broadcast([P, D_A])).then_inc(small_landed, 16)
            sp.dma_start(ln_gb[:, 1, :], a["ln_a_b"][l:l + 1, :].to_broadcast([P, D_A])).then_inc(small_landed, 16)
            sp.dma_start(qkg[:, 0, :], a["q_norm_g"][l:l + 1, :].to_broadcast([P, HD])).then_inc(small_landed, 16)
            sp.dma_start(qkg[:, 1, :], a["k_norm_g"][l:l + 1, :].to_broadcast([P, HD])).then_inc(small_landed, 16)
            for u in range(2, NU):
                w.load(sp, u)

        SMALL = 8 * 16

        @block.tensor
        def _(pe):
            pe.wait_ge(norm.scaled, TT)
            turn.pe(pe, lambda t, k: X[:, t, k * P:(k + 1) * P])
            pe.wait_ge(small_landed, SMALL)
            for h in range(H_A):
                mm = nc.tensor.transpose(prog.ps[:, 4 + h // 4, h % 4 * P:(h % 4 + 1) * P], wsR[:, h, :],
                                         prog.ident[:])
            mm.then_inc(ws_turned, 1)
            pe.wait_ge(turn.lo_done, turn.GROUPS)
            pe_rows_unit(prog, pe, w, 0, 0, acc_free, acc_ready, None, prog.hT_hi, prog.hT_lo)
            with pe.Fori(0, (NU - 1) // 2) as pair:
                for j in range(2):
                    unit = pair * 2 + 1 + j
                    pe_rows_unit(prog, pe, w, unit, (1 + j) % 2, acc_free, acc_ready, unit * TT,
                                 prog.hT_hi, prog.hT_lo)
            pe.wait_ge(ln_done, TT)
            pe.wait_ge(ws_taken, 2)
            for h in range(H_A):
                if h >= 4:
                    pe.wait_ge(ya_done, h - 3)
                nc.tensor.matmul(prog.ps[:, 4 + h % 4, :].rearrange("p (c d) -> p c d", c=TT), wsT[:, h, :],
                                 VA[:, :, h * HD:(h + 1) * HD], start=True, stop=True).then_inc(z_ready, 1)


        @block.scalar
        def _(act):
            norm.act(act, lambda e, t: e.wait_ge(x_landed[t // 2], 16))
            w.first_two(hi=act)
            act.wait_ge(small_landed, SMALL)
            turn.act(act)
            act.wait_ge(ws_turned, 1)
            for b in range(2):
                nc.scalar.copy(wsT[:, 4 * b:4 * b + 4, :], prog.ps[:, 4 + b, :].rearrange("p (h i) -> p h i", h=4)
                               ).then_inc(ws_taken, 1)
            for u, col in enumerate(order):
                for t in range(TT):
                    act.wait_ge(acc_ready, u * TT + t + 1)
                    c0 = order[u] % 512
                    if col == COL_KV:
                        dst, f = QKV[:, t, 512:768], ACT.Copy
                    elif COL_Q <= col < COL_KV:
                        dst, f = QKV[:, t, c0:c0 + UNIT], ACT.Copy
                    elif COL_VA <= col < COL_GA:
                        dst, f = VA[:, t, c0:c0 + UNIT], ACT.Copy
                    elif col < COL_VA:
                        dst, f = U[:, t, c0:c0 + UNIT], ACT.Copy
                    else:
                        dst, f = G[:, t, (u - 1) % 2 * UNIT:((u - 1) % 2 + 1) * UNIT], ACT.Silu
                        if col >= COL_GB:
                            act.wait_ge(ga_used, t + 1)
                    nc.scalar.activation(dst, prog.ps[:, t % 4, 0:UNIT], f).then_inc(acc_free, 1)
                if u + 2 < NU:
                    w.split_hi(act, u + 2)
                if u == 3:
                    act.wait_ge(head_sum, 2)
                    nc.scalar.activation(hst[:, 2, :, :], hst[:, 1, :, :], ACT.Sqrt).then_inc(head_root, 1)
                if u == 6:
                    act.wait_ge(ln_stat, 3)
                    nc.scalar.activation(rstd[:, 0, :], rstd[:, 1, :], ACT.Sqrt).then_inc(ln_root, 1)

        @block.vector
        def _(dve):
            norm.dve(dve)
            w.first_two(lo=dve)
            dve.wait_ge(small_landed, SMALL)
            turn.dve(dve)
            for u in range(NU):
                if u == 3:
                    for t in range(TT):
                        if t == 0:
                            dve.wait_ge(acc_free, 3 * TT)
                        if t:
                            dve.wait_ge(head_inv, t)
                        nc.vector.tensor_tensor(sq[:], QKV[:, t, 0:QKH * HD], QKV[:, t, 0:QKH * HD],
                                                ALU.mult).then_inc(head_sq, 1)
                        dve.wait_ge(head_sq, t + 1)
                        nc.vector.tensor_reduce(hst[:, 0, t, :], sq[:].rearrange("p (h d) -> p h d", d=HD), AX.X,
                                                ALU.add).then_inc(head_inv, 1)
                    dve.wait_ge(head_inv, TT)
                    nc.vector.tensor_scalar(hst[:, 1, :, :], hst[:, 0, :, :], 1.0 / HD, EPS, ALU.mult,
                                            ALU.add).then_inc(head_sum, 2)
                if u == 4:
                    dve.wait_ge(head_root, 1)
                    nc.vector.reciprocal(hst[:, 3, :, :], hst[:, 2, :, :]).then_inc(head_inv, 1)
                if u == 6:
                    dve.wait_ge(acc_free, 5 * TT)
                    for t in range(TT):
                        nc.vector.bn_stats(bn[:, t, :], VA[:, t, :]).then_inc(ln_step, 1)
                    for t in range(TT):
                        dve.wait_ge(ln_step, t + 1)
                        nc.vector.bn_aggr(mv[:, t, :], bn[:, t, :]).then_inc(ln_step, 1)
                    dve.wait_ge(ln_step, 2 * TT)
                    nc.vector.tensor_scalar(rstd[:, 1, :], mv[:, :, 1], 1.0, EPS, ALU.mult,
                                            ALU.add).then_inc(ln_stat, 3)
                if u == 8:
                    dve.wait_ge(ln_root, 1)
                    nc.vector.reciprocal(rstd[:, 1, :], rstd[:, 0, :]).then_inc(ln_step, 1)
                    dve.wait_ge(ln_step, 2 * TT + 1)
                    for t in range(TT):
                        nc.vector.tensor_scalar(VA[:, t, :], VA[:, t, :], mv[:, t, 0:1], rstd[:, 1, t:t + 1],
                                                ALU.subtract, ALU.mult).then_inc(ln_scaled, 1)
                if u + 2 < NU:
                    w.split_lo(dve, u + 2)
            dve.wait_ge(ga_used, TT)
            for h in range(H_A):
                dve.wait_ge(z_ready, h + 1)
                nc.vector.scalar_tensor_tensor(U[:, :, h * HD:(h + 1) * HD],
                                               prog.ps[:, 4 + h % 4, :].rearrange("p (c d) -> p c d", c=TT),
                                               spb[:, h:h + 1], U[:, :, h * HD:(h + 1) * HD], ALU.add,
                                               ALU.mult).then_inc(ya_done, 1)

        @block.gpsimd
        def _(pool):
            n = 0
            pool.wait_ge(small_landed, SMALL)
            pool.wait_ge(head_inv, TT + 1)

            def step(ins):
                nonlocal n
                n += 1
                ins.then_inc(rope_step, 1)

            def after():
                pool.wait_ge(rope_step, n)

            for t in range(TT):
                qk = QKV[:, t, 0:QKH * HD]
                heads = qk.rearrange("p (h d) -> p h d", d=HD)
                pairs = qk.rearrange("p (m b e) -> p m b e", b=2, e=16)
                rp = rot[:].rearrange("p (m b e) -> p m b e", b=2, e=16)
                rh = rot[:].rearrange("p (h d) -> p h d", d=HD)
                sgn = rope[:, 1, t, :].rearrange("p (a b e) -> p a b e", a=2, b=2)
                step(nc.gpsimd.tensor_tensor(heads, heads, hst[:, 3, t, :].unsqueeze(2).to_broadcast([P, QKH, HD]),
                                             ALU.mult))
                after()
                step(nc.gpsimd.tensor_tensor(heads[:, 0:H_B, :], heads[:, 0:H_B, :],
                                             qkg[:, 0, :].unsqueeze(1).to_broadcast([P, H_B, HD]), ALU.mult))
                step(nc.gpsimd.tensor_tensor(heads[:, H_B:, :], heads[:, H_B:, :],
                                             qkg[:, 1, :].unsqueeze(1).to_broadcast([P, KV, HD]), ALU.mult))
                after()
                for x in range(2):
                    for b in range(2):
                        h4 = rh[:, :, 32 * x + 16 * b:32 * x + 16 * b + 16]
                        o4 = heads[:, :, 32 * x + 16 * (1 - b):32 * x + 16 * (1 - b) + 16]
                        sn = sgn[:, x, b, :].unsqueeze(1).to_broadcast([P, QKH, 16])
                        step(nc.gpsimd.tensor_tensor(h4, o4, sn, ALU.mult))
                after()
                step(nc.gpsimd.tensor_tensor(heads, heads, rope[:, 0, t, :].unsqueeze(1).to_broadcast([P, QKH, HD]),
                                             ALU.mult))
                after()
                step(nc.gpsimd.tensor_tensor(qk, qk, rot[:], ALU.add))
                after()
            for t in range(TT):
                pool.wait_ge(ln_scaled, t + 1)
                step(nc.gpsimd.tensor_tensor(VA[:, t, :], VA[:, t, :], ln_gb[:, 0, :], ALU.mult))
                after()
                nc.gpsimd.tensor_tensor(VA[:, t, :], VA[:, t, :], ln_gb[:, 1, :], ALU.add).then_inc(ln_done, 1)
            pool.wait_ge(acc_free, 9 * TT)
            for t in range(TT):
                nc.gpsimd.tensor_tensor(U[:, t, :], U[:, t, :], G[:, t, :], ALU.mult).then_inc(ga_used, 1)
    return QKV, U, G


def attention(prog, l, QKV, G):
    nc = prog.nc
    QT_hi = prog.at("QT_hi", [P, 2, SEQ], 0, F32R)
    QT_lo = prog.at("QT_lo", [P, 2, SEQ], 8, F32R)
    KT_st = prog.at("KT_st", [P, KV, SEQ], 16, F32R)
    KT_hi = prog.at("KT_hi", [P, SEQ], 24, F32R)
    PR = prog.at("PR", [P, 2, SEQ], 32)
    PT = prog.at("PT", [P, 2, TT, P], 40)
    TWICE = prog.at("TWICE", [P, 2, TT, 2 * HD], 50)
    mx = prog.at("mx", [P, 64], 48)
    nmx = prog.at("nmx", [P, 64], 48.25)
    sm = prog.at("sm", [P, 64], 48.5)
    inv = prog.at("inv", [P, 64], 48.75)
    NT = H_B * TT
    SCALE = HD ** -0.5

    doubled = prog.sem("doubled")
    turned = prog.sem("turned")
    k_top = prog.sem("k_top")
    hi_done = prog.sem("hi_done")
    lo_done = prog.sem("lo_done")
    s_ready = prog.sem("s_ready")
    max_done = prog.sem("max_done")
    neg_done = prog.sem("neg_done")
    exp_done = prog.sem("exp_done")
    p_turned = prog.sem("p_turned")
    pt_a = prog.sem("pt_taken_a")
    pt_b = prog.sem("pt_taken_b")
    o_ready = prog.sem("o_ready")
    inv_done = prog.sem("inv_done")
    o_done = prog.sem("o_done")

    with nc.Block() as block:
        @block.tensor
        def _(pe):
            def turn_head(item):
                pe.wait_ge(doubled, item + 1)
                for half in range(2):
                    n = 2 * item + half
                    if n >= 2:
                        pe.wait_ge(lo_done, n - 1)
                    for j in range(4):
                        mm = nc.tensor.transpose(prog.ps[:, 6 + half, j * P:(j + 1) * P],
                                                 TWICE[:, item % 2, half * 4 + j, :], prog.ident[:])
                    mm.then_inc(turned, 1)

            def scores(n):
                head, t = n // TT, n % TT
                if t == 0:
                    pe.wait_ge(lo_done, 2 * (KV + head) + 2)
                    pe.wait_ge(k_top, 2 * KV)
                if n >= 2:
                    pe.wait_ge(exp_done, n - 1)
                for half in range(2):
                    keys = KT_st[:, head // (H_B // KV), half * 512:(half + 1) * 512]
                    out = prog.ps[:, 2 * (n % 2) + half, :]
                    nc.tensor.matmul(out, QT_hi[:, head % 2, t * P:(t + 1) * P], keys, start=True, stop=False)
                    mm = nc.tensor.matmul(out, QT_lo[:, head % 2, t * P:(t + 1) * P], keys, start=False, stop=True)
                mm.then_inc(s_ready, 1)

            def turn_p(n):
                pe.wait_ge(exp_done, n + 1)
                for half in range(2):
                    if n >= 1:
                        pe.wait_ge(pt_a if half == 0 else pt_b, n)
                    for j in range(4):
                        k = half * 4 + j
                        mm = nc.tensor.transpose(prog.ps[:, 4 + half, j * P:(j + 1) * P],
                                                 PR[:, n % 2, k * P:(k + 1) * P], prog.ident[:])
                    mm.then_inc(p_turned, 1)

            def values(n):
                head = n // TT
                g = head // (H_B // KV)
                if n >= 1:
                    pe.wait_ge(o_done, n)
                pe.wait_ge(pt_a, n + 1)
                pe.wait_ge(pt_b, n + 1)
                for k in range(TT):
                    mm = nc.tensor.matmul(prog.ps[:, 7, 256:256 + HD], PT[:, n % 2, k, :],
                                          QKV[:, k, 640 + g * HD:640 + (g + 1) * HD], start=(k == 0),
                                          stop=(k == TT - 1))
                mm.then_inc(o_ready, 1)

            for item in range(KV + 1):
                turn_head(item)
            for n in range(NT + 1):
                if n < NT:
                    scores(n)
                if n >= 1:
                    turn_p(n - 1)
                    values(n - 1)
                if n % TT == 1 and n // TT + 1 < H_B:
                    pe.wait_ge(o_done, n)
                    turn_head(KV + n // TT + 1)

        @block.scalar
        def _(act):
            for i in range(2 * KV):
                act.wait_ge(turned, i + 1)
                cols = slice(i % 2 * 512, (i % 2 + 1) * 512)
                nc.scalar.activation(KT_st[0:HD, i // 2, cols], prog.ps[0:HD, 6 + i % 2, :],
                                     ACT.Copy).then_inc(k_top, 1)
                if i >= 2:
                    act.wait_ge(lo_done, i - 1)
                nc.scalar.activation(KT_hi[HD:P, cols], prog.ps[HD:P, 6 + i % 2, :], ACT.Copy).then_inc(hi_done, 1)

            def q_split(head):
                for half in range(2):
                    n = 2 * (KV + head) + half
                    act.wait_ge(turned, n + 1)
                    nc.scalar.activation(QT_hi[:, head % 2, half * 512:(half + 1) * 512], prog.ps[:, 6 + half, :],
                                         ACT.Copy).then_inc(hi_done, 1)

            q_split(0)
            for n in range(NT + 1):
                if n < NT:
                    act.wait_ge(neg_done, n + 1)
                    if n >= 2:
                        act.wait_ge(p_turned, 2 * n - 2)
                    nc.scalar.activation(PR[:, n % 2, :].rearrange("p (a b) -> p a b", a=2),
                                         prog.ps[:, 2 * (n % 2):2 * (n % 2) + 2, :], ACT.Exp,
                                         bias=nmx[:, n:n + 1], scale=SCALE,
                                         accum_out=sm[:, n:n + 1]).then_inc(exp_done, 1)
                if n >= 1:
                    m = n - 1
                    act.wait_ge(p_turned, 2 * m + 1)
                    if m >= 2:
                        act.wait_ge(o_ready, m - 1)
                    nc.scalar.activation(PT[:, m % 2, 0:4, :], prog.ps[:, 4, :].rearrange("p (a b) -> p a b", a=4),
                                         ACT.Copy).then_inc(pt_a, 1)
                if n % TT == 1 and n // TT + 1 < H_B:
                    q_split(n // TT + 1)

        @block.gpsimd
        def _(pool):
            for item in range(KV + H_B):
                head = H_B + item if item < KV else item - KV
                if item >= 2:
                    pool.wait_ge(turned, 2 * item - 2)
                src = QKV[:, :, head * HD:(head + 1) * HD]
                nc.gpsimd.tensor_copy(TWICE[:, item % 2, :, 0:HD], src)
                nc.gpsimd.tensor_copy(TWICE[:, item % 2, :, HD:], src).then_inc(doubled, 1)

        @block.vector
        def _(dve):
            for i in range(2 * KV):
                dve.wait_ge(hi_done, i + 1)
                nc.vector.tensor_tensor(KT_st[HD:P, i // 2, i % 2 * 512:(i % 2 + 1) * 512], prog.ps[HD:P, 6 + i % 2, :],
                                        plane(KT_hi[HD:P, i % 2 * 512:(i % 2 + 1) * 512]),
                                        ALU.subtract).then_inc(lo_done, 1)

            def q_split(head):
                for half in range(2):
                    dve.wait_ge(hi_done, 2 * (KV + head) + half + 1)
                    cols = slice(half * 512, (half + 1) * 512)
                    nc.vector.tensor_tensor(QT_lo[:, head % 2, cols], prog.ps[:, 6 + half, :],
                                            plane(QT_hi[:, head % 2, cols]), ALU.subtract).then_inc(lo_done, 1)

            q_split(0)
            for n in range(NT + 1):
                if n < NT:
                    dve.wait_ge(s_ready, n + 1)
                    nc.vector.tensor_reduce(mx[:, n:n + 1], prog.ps[:, 2 * (n % 2):2 * (n % 2) + 2, :], AX.XY,
                                            ALU.max).then_inc(max_done, 1)
                    dve.wait_ge(max_done, n + 1)
                    nc.vector.tensor_scalar(nmx[:, n:n + 1], mx[:, n:n + 1], -SCALE, None,
                                            ALU.mult).then_inc(neg_done, 1)
                if n >= 1:
                    m = n - 1
                    head, t = m // TT, m % TT
                    dve.wait_ge(p_turned, 2 * m + 2)
                    if m >= 2:
                        dve.wait_ge(o_ready, m - 1)
                    nc.vector.tensor_copy(PT[:, m % 2, 4:8, :], prog.ps[:, 5, :].rearrange("p (a b) -> p a b", a=4)
                                          ).then_inc(pt_b, 1)
                    dve.wait_ge(exp_done, m + 1)
                    nc.vector.reciprocal(inv[:, m:m + 1], sm[:, m:m + 1]).then_inc(inv_done, 1)
                    dve.wait_ge(inv_done, m + 1)
                    dve.wait_ge(o_ready, m + 1)
                    dst = G[:, t, head * HD:(head + 1) * HD]
                    nc.vector.scalar_tensor_tensor(dst, prog.ps[:, 7, 256:256 + HD], inv[:, m:m + 1], dst, ALU.mult,
                                                   ALU.mult).then_inc(o_done, 1)
                if n % TT == 1 and n // TT + 1 < H_B:
                    q_split(n // TT + 1)


def output_rows(prog, w_rows, post_g, src, x_src, x_dst, O):
    nc = prog.nc
    kb = prog.B
    pg = prog.at("pg", [P, D], kb + 72)
    xin = prog.at("xin", [P, 2, D], kb + 80)
    stat = prog.at("stat", [P, 64], kb + 76)
    NU = D // UNIT
    wv = w_rows.rearrange("(k p) n -> p k n", p=P)

    def wsrc(u, raw):
        return [(raw.rearrange("p (k n) -> p k n", k=KT), wv[:, :, u * UNIT:(u + 1) * UNIT])]

    acc_ready = prog.sem("acc_ready")
    w = Weights(prog, wsrc, acc_ready, TT)
    turn = Turn(prog, gain=False)
    acc_free = prog.sem("acc_free")
    pg_landed = prog.sem("pg_landed")
    x_landed = [prog.sem("x_landed0"), prog.sem("x_landed1")]
    squared = prog.sem("squared")
    meaned = prog.sem("meaned")
    rooted = prog.sem("rooted")
    inverted = prog.sem("inverted")
    normed = prog.sem("normed")
    x_done = prog.sem("x_done")
    stored = prog.sem("stored")
    xv = x_src.rearrange("(t p) d -> p t d", p=P)
    ov = x_dst.rearrange("(t p) d -> p t d", p=P)


    with nc.Block() as block:
        @block.sync
        def _(sp):
            w.first_two(load=sp)
            if post_g is not None:
                sp.dma_start(pg[:], post_g.to_broadcast([P, D])).then_inc(pg_landed, 16)
            for t in range(2):
                sp.dma_start(xin[:, t, :], xv[:, t, :]).then_inc(x_landed[t], 16)
            for u in range(2, NU):
                w.load(sp, u)
            for t in range(TT):
                sp.wait_ge(x_done, t + 1)
                sp.dma_start(ov[:, t, :], O[:, t, :]).then_inc(stored, 16)
                if t + 2 < TT:
                    sp.dma_start(xin[:, t % 2, :], xv[:, t + 2, :]).then_inc(x_landed[t % 2], 16)
            sp.wait_ge(stored, 16 * TT)

        @block.tensor
        def _(pe):
            turn.pe(pe, src)
            pe.wait_ge(turn.lo_done, turn.GROUPS)
            pe_rows_unit(prog, pe, w, 0, 0, acc_free, acc_ready, None, prog.hT_hi, prog.hT_lo)
            for u in range(1, NU):
                pe_rows_unit(prog, pe, w, u, u % 2, acc_free, acc_ready, u * TT, prog.hT_hi, prog.hT_lo)

        @block.scalar
        def _(act):
            w.first_two(hi=act)
            turn.act(act)
            for u in range(NU):
                for t in range(TT):
                    act.wait_ge(acc_ready, u * TT + t + 1)
                    nc.scalar.activation(O[:, t, u * UNIT:(u + 1) * UNIT], prog.ps[:, t % 4, 0:UNIT],
                                         ACT.Copy).then_inc(acc_free, 1)
                if u + 2 < NU:
                    w.split_hi(act, u + 2)
            if post_g is not None:
                for t in range(TT):
                    act.wait_ge(acc_free, NU * TT)
                    nc.scalar.activation(prog.ps[:, 4 + t % 2 * 2:6 + t % 2 * 2, :],
                                         O[:, t, :].rearrange("p (a b) -> p a b", a=2), ACT.Square,
                                         accum_out=stat[:, t:t + 1]).then_inc(squared, 1)
                    act.wait_ge(squared, t + 1)
                act.wait_ge(meaned, 1)
                nc.scalar.activation(stat[:, 8:16], stat[:, 16:24], ACT.Sqrt).then_inc(rooted, 1)

        @block.vector
        def _(dve):
            w.first_two(lo=dve)
            turn.dve(dve)
            for u in range(2, NU):
                w.split_lo(dve, u)
            if post_g is not None:
                dve.wait_ge(pg_landed, 16)
                dve.wait_ge(squared, TT)
                nc.vector.tensor_scalar(stat[:, 16:24], stat[:, 0:8], 1.0 / D, EPS, ALU.mult,
                                        ALU.add).then_inc(meaned, 1)
                dve.wait_ge(rooted, 1)
                nc.vector.reciprocal(stat[:, 24:32], stat[:, 8:16]).then_inc(inverted, 1)
                dve.wait_ge(inverted, 1)
            else:
                dve.wait_ge(acc_free, NU * TT)
            for t in range(TT):
                if post_g is not None:
                    nc.vector.scalar_tensor_tensor(O[:, t, :], O[:, t, :], stat[:, 24 + t:25 + t], pg[:], ALU.mult,
                                                   ALU.mult).then_inc(normed, 1)
                    dve.wait_ge(normed, t + 1)
                dve.wait_ge(x_landed[t % 2], 16 * (t // 2 + 1))
                nc.vector.tensor_tensor(O[:, t, :], O[:, t, :], xin[:, t % 2, :], ALU.add).then_inc(x_done, 1)


def pe_columns_unit(prog, pe, w, unit, slot, waits, acc_ready, bank):
    nc = prog.nc
    pe.wait_ge(w.lo_ready, unit + 1)
    for i in range(4):
        j, half = i // 2, i % 2
        if waits is not None:
            waits(i)
        for k in range(KT):
            wc = slice(k * UNIT + j * P, k * UNIT + (j + 1) * P)
            tok = slice(half * 512, (half + 1) * 512)
            mm = three_products(nc, prog.ps[:, bank + i, :], prog.w_hi[:, slot, wc], prog.w_lo[:, slot, wc],
                                prog.hT_hi[:, k, tok], prog.hT_lo[:, k, tok], k == 0, k == KT - 1)
        mm.then_inc(acc_ready, 1)


def gla_inputs(prog, a, x_src):
    nc = prog.nc
    kb = prog.B
    X = prog.at("X", [P, TT, D], kb)
    junk = prog.at("junk", [P, D], kb + 80)
    Q = prog.at("Qd", [P, GH, SEQ], kb)
    K = prog.at("Kd", [P, GH, SEQ], kb + 16)
    B = prog.at("Bc", [P, GH, SEQ], kb + 32)
    V = prog.at("V", [P, TT, GH * DV], kb + 48)
    E = prog.at("E", [P, GH, SEQ], kb + 48)
    wa_raw = prog.at("wa_raw", [P, KT, P], kb + 64)
    wa_hi = prog.at("wa_hi", [P, KT, P], kb + 68, F32R)
    wa_lo = prog.at("wa_lo", [P, KT, P], kb + 72, F32R)
    AL = prog.at("AL", [RANK, SEQ], kb + 76)
    tmp = prog.at("tmp", [P, 2, 512], kb + 80)
    keep = prog.at("keep", [P, SEQ], kb + 84)
    wau = prog.at("wau", [RANK, GH * DK], kb + 88)
    ba = prog.at("ba", [P, GH], kb + 90)
    DEC = prog.at("DEC", [P, GH, SEQ // CH], kb + 92)
    stat = prog.at("stat", [P, 64], kb + 90.75)
    order = [0, UNIT, 512, 512 + UNIT] + [1024 + UNIT * i for i in range(4)]
    NU = len(order)
    COLS = 4
    wv = a["gla_w_in"].rearrange("(k p) n -> p k n", p=P)

    def src(u, raw):
        return [(raw.rearrange("p (k n) -> p k n", k=KT), wv[:, :, order[u]:order[u] + UNIT])]

    acc_ready = prog.sem("acc_ready")

    def sums(u):
        return 4 * (u + 1) if u < COLS else 4 * COLS + TT * (u + 1 - COLS)

    w = Weights(prog, src, acc_ready, 4)
    turn = Turn(prog)
    norm = RowNorm(prog, X, junk, stat)
    x_landed = [prog.sem(f"x_landed{i}") for i in range(4)]
    small_landed = prog.sem("small_landed")
    acc_free = prog.sem("acc_free")
    wa_zero = prog.sem("wa_zero")
    wa_landed = prog.sem("wa_landed")
    wa_split = prog.sem("wa_split")
    wa_done = prog.sem("wa_done")
    al_ready = prog.sem("al_ready")
    al_taken = prog.sem("al_taken")
    z_ready = prog.sem("z_ready")
    z_abs = prog.sem("z_abs")
    z_exp = prog.sem("z_exp")
    z_min = prog.sem("z_min")
    z_log = prog.sem("z_log")
    keep_made = prog.sem("keep_made")
    ls_done = prog.sem("ls_done")
    b_done = prog.sem("b_done")
    e_done = prog.sem("e_done")
    Bv = B[:].rearrange("p h (c s) -> p h c s", s=CH)

    with nc.Block() as block:
        @block.sync
        def _(sp):
            sp.dma_start(prog.gain[:], a["norm1"].rearrange("(k p) -> p k", p=P),
                         allow_slow_non_contiguous=True).then_inc(small_landed, 16)
            xv = x_src.rearrange("(t p) d -> p t d", p=P)
            for t in range(0, TT, 2):
                sp.dma_start(X[:, t:t + 2, :], xv[:, t:t + 2, :]).then_inc(x_landed[t // 2], 16)
            w.first_two(load=sp)
            sp.dma_start(wau[:], a["gla_w_alpha_up"]).then_inc(small_landed, 16)
            sp.dma_start(ba[:], a["gla_b_alpha"].rearrange("(h p) -> p h", p=P),
                         allow_slow_non_contiguous=True).then_inc(small_landed, 16)
            sp.wait_ge(wa_zero, 1)
            sp.dma_start(wa_raw[:, :, 0:RANK], wv[:, :, 3072:3072 + RANK]).then_inc(wa_landed, 16)
            for u in range(2, NU):
                w.load(sp, u)

        SMALL = 3 * 16

        @block.gpsimd
        def _(pool):
            nc.gpsimd.memset(wa_raw[:], 0.0).then_inc(wa_zero, 1)
            nc.gpsimd.memset(keep[:], 1.0).then_inc(keep_made, 1)
            pool.wait_ge(keep_made, 1)
            nc.gpsimd.memset(keep[:].rearrange("p (c s) -> p c s", s=CH)[:, :, 0], 0.0).then_inc(keep_made, 1)

        @block.tensor
        def _(pe):
            pe.wait_ge(norm.scaled, TT)
            turn.pe(pe, lambda t, k: X[:, t, k * P:(k + 1) * P])
            pe.wait_ge(turn.lo_done, turn.GROUPS)
            pe.wait_ge(wa_split, 2)
            for half in range(2):
                tok = slice(half * 512, (half + 1) * 512)
                for k in range(KT):
                    mm = three_products(nc, prog.ps[:, 4 + half, :], wa_hi[:, k, :], wa_lo[:, k, :],
                                        prog.hT_hi[:, k, tok], prog.hT_lo[:, k, tok], k == 0, k == KT - 1)
                mm.then_inc(al_ready, 1)
            pe_columns_unit(prog, pe, w, 0, 0, None, acc_ready, 0)
            pe.wait_ge(al_taken, 2)
            pe.wait_ge(small_landed, SMALL)
            for n in range(2 * GH):
                h, half = n // 2, n % 2
                if n >= 4:
                    pe.wait_ge(z_abs, n - 3)
                    pe.wait_ge(z_min, n - 3)
                nc.tensor.matmul(prog.ps[:, 4 + n % 4, :], wau[:, h * DK:(h + 1) * DK],
                                 AL[:, half * 512:(half + 1) * 512], start=True, stop=True).then_inc(z_ready, 1)
            for u in range(1, COLS):
                pe_columns_unit(prog, pe, w, u, u % 2, lambda i, u=u: pe.wait_ge(acc_free, 4 * (u - 1) + i + 1),
                                acc_ready, 0)
            for u in range(COLS, NU):
                pe_rows_unit(prog, pe, w, u, u % 2, acc_free, acc_ready, 4 * COLS + TT * (u - COLS),
                             prog.hT_hi, prog.hT_lo)

        @block.scalar
        def _(act):
            norm.act(act, lambda e, t: e.wait_ge(x_landed[t // 2], 16))
            w.first_two(hi=act)
            act.wait_ge(small_landed, SMALL)
            turn.act(act)
            act.wait_ge(wa_landed, 16)
            nc.scalar.activation(wa_hi[:], wa_raw[:], ACT.Copy).then_inc(wa_split, 1)
            for half in range(2):
                act.wait_ge(al_ready, half + 1)
                nc.scalar.activation(AL[:, half * 512:(half + 1) * 512], prog.ps[0:RANK, 4 + half, :],
                                     ACT.Copy).then_inc(al_taken, 1)
            for n in range(2 * GH):
                h, half = n // 2, n % 2
                act.wait_ge(z_ready, n + 1)
                if n >= 2:
                    act.wait_ge(z_exp, n - 1)
                nc.scalar.activation(tmp[:, n % 2, :], prog.ps[:, 4 + n % 4, :], ACT.Abs,
                                     bias=ba[:, h:h + 1]).then_inc(z_abs, 1)
                act.wait_ge(z_abs, n + 1)
                nc.scalar.activation(B[:, h, half * 512:(half + 1) * 512], tmp[:, n % 2, :], ACT.Exp,
                                     scale=-1.0).then_inc(z_exp, 1)
            act.wait_ge(z_exp, 2 * GH)
            for h in range(GH):
                nc.scalar.activation(B[:, h, :], B[:, h, :], ACT.Ln, bias=1.0).then_inc(z_log, 1)
            for h in range(GH):
                act.wait_ge(b_done, h + 1)
                nc.scalar.activation(E[:, h, :], B[:, h, :], ACT.Exp, scale=1.0 / TAU).then_inc(e_done, 1)
            nc.scalar.activation(DEC[:], Bv[:, :, :, CH - 1], ACT.Exp, scale=1.0 / TAU).then_inc(e_done, 1)
            act.wait_ge(e_done, GH + 1)
            for h in range(GH):
                nc.scalar.activation(B[:, h, :], B[:, h, :], ACT.Exp, scale=-1.0 / TAU).then_inc(e_done, 1)
            w.per_unit = 1
            for u in range(NU):
                if u >= COLS:
                    for t in range(TT):
                        act.wait_ge(acc_ready, sums(u - 1) + t + 1)
                        if u == COLS and t == 0:
                            act.wait_ge(acc_free, 4 * COLS)
                        nc.scalar.activation(V[:, t, (u - COLS) * UNIT:(u - COLS + 1) * UNIT],
                                             prog.ps[:, t % 4, 0:UNIT], ACT.Copy).then_inc(acc_free, 1)
                if u + 2 < NU:
                    act.wait_ge(acc_ready, sums(u))
                    w.split_hi(act, u + 2, reused=False)

        @block.vector
        def _(dve):
            norm.dve(dve)
            w.first_two(lo=dve)
            dve.wait_ge(small_landed, SMALL)
            turn.dve(dve)
            dve.wait_ge(wa_split, 1)
            nc.vector.tensor_tensor(wa_lo[:], wa_raw[:], plane(wa_hi[:]), ALU.subtract).then_inc(wa_split, 1)
            for n in range(2 * GH):
                h, half = n // 2, n % 2
                dve.wait_ge(z_abs, n + 1)
                nc.vector.tensor_scalar(K[:, h, half * 512:(half + 1) * 512], prog.ps[:, 4 + n % 4, :],
                                        ba[:, h:h + 1], 0.0, ALU.add, ALU.min).then_inc(z_min, 1)
            dve.wait_ge(keep_made, 2)
            for h in range(GH):
                dve.wait_ge(z_log, h + 1)
                dve.wait_ge(z_min, 2 * GH)
                nc.vector.tensor_tensor(K[:, h, :], K[:, h, :], B[:, h, :], ALU.subtract).then_inc(ls_done, 1)
                dve.wait_ge(ls_done, h + 1)
                nc.vector.tensor_tensor_scan(B[:, h, :], keep[:], K[:, h, :], 0.0, ALU.mult,
                                             ALU.add).then_inc(b_done, 1)
            for u in range(COLS):
                for i in range(4):
                    j, half = i // 2, i % 2
                    h = (u % 2) * 2 + j
                    tok = slice(half * 512, (half + 1) * 512)
                    dve.wait_ge(acc_ready, 4 * u + i + 1)
                    if u < 2:
                        dve.wait_ge(e_done, GH)
                        nc.vector.scalar_tensor_tensor(Q[:, h, tok], prog.ps[:, i, :], DK ** -0.5, E[:, h, tok],
                                                       ALU.mult, ALU.mult).then_inc(acc_free, 1)
                    else:
                        dve.wait_ge(e_done, 2 * GH + 1)
                        dve.wait_ge(b_done, GH)
                        nc.vector.tensor_tensor(K[:, h, tok], prog.ps[:, i, :], B[:, h, tok],
                                                ALU.mult).then_inc(acc_free, 1)
                w.split_lo(dve, u + 2)
            for u in range(COLS + 2, NU):
                w.split_lo(dve, u)
    return Q, K, V, DEC


def gla_core(prog, a, Q, K, V, DEC):
    nc = prog.nc
    kb = prog.B
    NCH = SEQ // CH
    f = kb + 32
    S = prog.at("S", [P, 2, GH, P], f)
    KE = prog.at("KE", [P, 2, GH, P], f + 4)
    KEt = prog.at("KEt", [P, 2, GH, P], f + 8)
    stat = prog.at("stat", [P, 3, TT, GH], f + 12)
    gat = prog.at("gat", [P, 2, UNIT], f + 13)
    ST = prog.at("ST", [P, 2, GH, DV], kb + 80)
    mask = prog.at("mask", [P, P], f + 15, U32)
    on = prog.at("on", [P, GH * DV], kb + 88)
    junk = prog.at("junk", [P, DV], kb + 92.5)
    wv = a["gla_w_in"].rearrange("(k p) n -> p k n", p=P)
    NU = 4

    def src(u, raw):
        return [(raw.rearrange("p (k n) -> p k n", k=KT), wv[:, :, 2048 + u * UNIT:2048 + (u + 1) * UNIT])]

    acc_ready = prog.sem("acc_ready")
    w = Weights(prog, src, acc_ready, TT)
    small_landed = prog.sem("small_landed")
    zeroed = prog.sem("zeroed")
    masked = prog.sem("masked")
    st_zero = prog.sem("st_zero")
    s_ready = prog.sem("s_ready")
    s_done = prog.sem("s_done")
    ke_done = prog.sem("ke_done")
    ke_turned = prog.sem("ke_turned")
    ke_taken = prog.sem("ke_taken")
    kv_ready = prog.sem("kv_ready")
    st_done = prog.sem("st_done")
    inter = prog.sem("inter")
    o_ready = prog.sem("o_ready")
    squared = prog.sem("squared")
    meaned = prog.sem("meaned")
    rooted = prog.sem("rooted")
    inverted = prog.sem("inverted")
    o_done = prog.sem("o_done")
    acc_free = prog.sem("acc_free")
    y_done = prog.sem("y_done")

    with nc.Block() as block:
        @block.sync
        def _(sp):
            w.first_two(load=sp)
            sp.dma_start(on[:], a["gla_out_norm"].rearrange("(o n) -> o n", o=1).to_broadcast([P, GH * DV])
                         ).then_inc(small_landed, 16)
            for u in range(2, NU):
                w.load(sp, u)

        @block.gpsimd
        def _(pool):
            nc.gpsimd.memset(mask[:].bitcast(F32), 1.0).then_inc(zeroed, 1)
            nc.gpsimd.memset(S[:], 0.0).then_inc(zeroed, 1)
            pool.wait_ge(zeroed, 2)
            nc.gpsimd.affine_select(out=mask[:].bitcast(F32), in_=mask[:].bitcast(F32), compare_op=ALU.is_ge,
                                    fill=0.0, base=0, pattern=[[1, P]], channel_multiplier=-1).then_inc(masked, 1)
            pool.wait_ge(masked, 1)
            nc.gpsimd.memset(mask[0:CH, CH:P].bitcast(F32), 0.0).then_inc(masked, 1)
            for t in range(TT):
                if t >= 2:
                    pool.wait_ge(ke_turned, t - 1)
                out = KE[:, t % 2, :, :].rearrange("p h (c s) -> p h c s", s=CH)
                k_in = K[:, :, t * P:(t + 1) * P].rearrange("p h (c s) -> p h c s", s=CH)
                for c in range(2):
                    ins = nc.gpsimd.tensor_tensor(out[:, :, c, :], k_in[:, :, c, :],
                                                  DEC[:, :, 2 * t + c].unsqueeze(2).to_broadcast([P, GH, CH]),
                                                  ALU.mult)
                    ins.then_inc(ke_done, 1)

        @block.tensor
        def _(pe):
            def tile_scores(t):
                if t >= 1:
                    pe.wait_ge(s_done, t)
                for h in range(GH):
                    mm = nc.tensor.matmul(prog.ps[:, 0, h * P:(h + 1) * P], K[:, h, t * P:(t + 1) * P],
                                          Q[:, h, t * P:(t + 1) * P], start=(h == 0), stop=True,
                                          skip_group_check=True)
                mm.then_inc(s_ready, 1)
                pe.wait_ge(ke_done, 2 * t + 2)
                if t >= 1:
                    pe.wait_ge(ke_taken, t)
                for h in range(GH):
                    mm = nc.tensor.transpose(prog.ps[:, 1, h * P:(h + 1) * P], KE[:, t % 2, h, :], prog.ident[:])
                mm.then_inc(ke_turned, 1)

            def keys_values(t, c):
                n = 2 * t + c
                if n >= 1:
                    pe.wait_ge(st_done, GH * n)
                rows = slice(c * CH, (c + 1) * CH)
                for h in range(GH):
                    mm = nc.tensor.matmul(prog.ps[:, 2 + h // 2, h % 2 * DV:(h % 2 + 1) * DV], KEt[rows, t % 2, h, :],
                                          V[rows, t, h * DV:(h + 1) * DV], start=(h % 2 == 0), stop=True,
                                          skip_group_check=True)
                mm.then_inc(kv_ready, 1)

            def outs(t, h):
                return prog.ps[:, 4 + 2 * (t % 2) + h // 2, h % 2 * DV:(h % 2 + 1) * DV]

            def within(t):
                pe.wait_ge(s_done, t + 1)
                if t >= 2:
                    pe.wait_ge(o_done, GH * (t - 1))
                for h in range(GH):
                    nc.tensor.matmul(outs(t, h), S[:, t % 2, h, :], V[:, t, h * DV:(h + 1) * DV],
                                     start=(h % 2 == 0), stop=False, skip_group_check=True)

            def from_state(t, c):
                n = 2 * t + c
                if n:
                    pe.wait_ge(st_done, GH * n)
                for h in range(GH):
                    cols = slice(t * P + c * CH, t * P + (c + 1) * CH)
                    mm = nc.tensor.matmul(outs(t, h)[c * CH:(c + 1) * CH], Q[:, h, cols], ST[:, n % 2, h, :],
                                          start=False, stop=True, skip_group_check=True)
                mm.then_inc(inter, 1)

            pe.wait_ge(st_zero, 1)
            tile_scores(0)
            for t in range(TT):
                pe.wait_ge(ke_taken, t + 1)
                keys_values(t, 0)
                within(t)
                from_state(t, 0)
                if t + 1 < TT:
                    tile_scores(t + 1)
                keys_values(t, 1)
                from_state(t, 1)
            pe.wait_ge(st_done, GH * NCH)
            pe_rows_unit(prog, pe, w, 0, 0, acc_free, acc_ready, None, prog.hT_hi, prog.hT_lo)
            for u in range(1, NU):
                pe_rows_unit(prog, pe, w, u, u % 2, acc_free, acc_ready, u * TT, prog.hT_hi, prog.hT_lo)

        @block.scalar
        def _(act):
            def head_squares(t):
                act.wait_ge(inter, 2 * t + 2)
                for h in range(GH):
                    n = t * GH + h
                    if n:
                        act.wait_ge(squared, n)
                    nc.scalar.activation(junk[:], prog.ps[:, 4 + 2 * (t % 2) + h // 2, h % 2 * DV:(h % 2 + 1) * DV],
                                         ACT.Square, accum_out=stat[:, 0, t, h:h + 1]).then_inc(squared, 1)
                act.wait_ge(meaned, t + 1)
                nc.scalar.activation(stat[:, 2, t, :], stat[:, 1, t, :], ACT.Sqrt).then_inc(rooted, 1)

            w.first_two(hi=act)
            for t in range(TT):
                act.wait_ge(ke_turned, t + 1)
                if t >= 2:
                    act.wait_ge(kv_ready, 2 * t - 2)
                nc.scalar.activation(KEt[:, t % 2, :, :], prog.ps[:, 1, :].rearrange("p (h d) -> p h d", h=GH),
                                     ACT.Copy).then_inc(ke_taken, 1)
                if t >= 1:
                    head_squares(t - 1)
            head_squares(TT - 1)
            for u in range(NU):
                for t in range(TT):
                    n = u * TT + t
                    act.wait_ge(acc_ready, n + 1)
                    if n >= 2:
                        act.wait_ge(y_done, n - 1)
                    nc.scalar.activation(gat[:, n % 2, :], prog.ps[:, t % 4, 0:UNIT], ACT.Silu).then_inc(acc_free, 1)
                if u + 2 < NU:
                    w.split_hi(act, u + 2)

        @block.vector
        def _(dve):
            nc.vector.memset(ST[:, 0, :, :], 0.0).then_inc(st_zero, 1)
            dve.wait_ge(st_zero, 1)
            dve.wait_ge(zeroed, 2)
            dve.wait_ge(masked, 2)
            dve.wait_ge(small_landed, 16)
            w.first_two(lo=dve)

            def mask_scores(t):
                dve.wait_ge(s_ready, t + 1)
                if t >= 2:
                    dve.wait_ge(inter, 2 * t - 3)
                nc.vector.copy_predicated(S[:, t % 2, :, :], mask[:].unsqueeze(1).to_broadcast([P, GH, P]),
                                          prog.ps[:, 0, :].rearrange("p (h d) -> p h d", h=GH)).then_inc(s_done, 1)

            def state(t, c):
                n = 2 * t + c
                dve.wait_ge(kv_ready, n + 1)
                if n:
                    dve.wait_ge(inter, n)
                    dve.wait_ge(st_done, GH * n)
                for h in range(GH):
                    nc.vector.scalar_tensor_tensor(ST[:, (n + 1) % 2, h, :], ST[:, n % 2, h, :], DEC[:, h, n:n + 1],
                                                   prog.ps[:, 2 + h // 2, h % 2 * DV:(h % 2 + 1) * DV], ALU.mult,
                                                   ALU.add).then_inc(st_done, 1)

            def normed(t):
                dve.wait_ge(squared, GH * (t + 1))
                nc.vector.tensor_scalar(stat[:, 1, t, :], stat[:, 0, t, :], 1.0 / DV, EPS, ALU.mult,
                                        ALU.add).then_inc(meaned, 1)
                dve.wait_ge(rooted, t + 1)
                nc.vector.reciprocal(stat[:, 0, t, :], stat[:, 2, t, :]).then_inc(inverted, 1)
                dve.wait_ge(inverted, t + 1)
                for h in range(GH):
                    cols = slice(h * DV, (h + 1) * DV)
                    nc.vector.scalar_tensor_tensor(V[:, t, cols],
                                                   prog.ps[:, 4 + 2 * (t % 2) + h // 2, h % 2 * DV:(h % 2 + 1) * DV],
                                                   stat[:, 0, t, h:h + 1], on[:, cols], ALU.mult,
                                                   ALU.mult).then_inc(o_done, 1)

            mask_scores(0)
            for t in range(TT):
                state(t, 0)
                if t + 1 < TT:
                    mask_scores(t + 1)
                state(t, 1)
                if t >= 1:
                    normed(t - 1)
            normed(TT - 1)
            for u in range(NU):
                for t in range(TT):
                    n = u * TT + t
                    cols = slice(u * UNIT, (u + 1) * UNIT)
                    dve.wait_ge(acc_free, n + 1)
                    if n == 0:
                        dve.wait_ge(o_done, GH * TT)
                    nc.vector.tensor_tensor(V[:, t, cols], V[:, t, cols], gat[:, n % 2, :], ALU.mult).then_inc(y_done, 1)
                if u + 2 < NU:
                    w.split_lo(dve, u + 2)


def ffn_up(prog, a, x_src):
    nc = prog.nc
    kb = prog.B
    X = prog.at("X", [P, TT, D], kb)
    A = prog.at("A", [P, FT, SEQ], kb)
    junk = prog.at("junk", [P, D], kb + 40)
    stat = prog.at("stat", [P, 64], kb + 93)
    craw = prog.at("craw", [2 * FT, 4, P], kb + 48)
    CW = prog.at("CW", [P, 4, 2 * FT], kb + 92)
    CG = prog.at("CG", [P, SEQ], kb + 88)
    NU = FT
    wv = a["ffn_w_up"].rearrange("(k p) n -> p k n", p=P)

    def src(u, raw):
        raw = raw.rearrange("p (k n) -> p k n", k=KT)
        return [(raw[:, :, 0:P], wv[:, :, bass.ds(u * P, P)]),
                (raw[:, :, P:], wv[:, :, bass.ds(u * P + FFN, P)])]

    acc_ready = prog.sem("acc_ready")
    w = Weights(prog, src, acc_ready, 4, pieces=2)
    turn = Turn(prog)
    norm = RowNorm(prog, X, junk, stat)
    x_landed = [prog.sem(f"x_landed{i}") for i in range(4)]
    small_landed = prog.sem("small_landed")
    cw_turned = prog.sem("cw_turned")
    cw_taken = prog.sem("cw_taken")
    newest_tap = prog.sem("newest_tap")
    tap = prog.sem("tap")
    gate_done = prog.sem("gate_done")
    a_done = prog.sem("a_done")

    with nc.Block() as block:
        @block.sync
        def _(sp):
            sp.dma_start(prog.gain[:], a["norm2"].rearrange("(k p) -> p k", p=P),
                         allow_slow_non_contiguous=True).then_inc(small_landed, 16)
            xv = x_src.rearrange("(t p) d -> p t d", p=P)
            for t in range(0, TT, 2):
                sp.dma_start(X[:, t:t + 2, :], xv[:, t:t + 2, :]).then_inc(x_landed[t // 2], 16)
            w.first_two(load=sp)
            sp.dma_start(craw[:, 0:3, :], a["ffn_conv_w"].rearrange("j (f p) -> f j p", p=P)).then_inc(small_landed, 16)
            sp.dma_start(craw[:, 3, :], a["ffn_conv_b"].rearrange("(f p) -> f p", p=P)).then_inc(small_landed, 16)
            with sp.Fori(1, NU // 2) as pair:
                for slot in range(2):
                    w.load(sp, pair * 2 + slot, slot)

        SMALL = 3 * 16

        @block.tensor
        def _(pe):
            pe.wait_ge(norm.scaled, TT)
            turn.pe(pe, lambda t, k: X[:, t, k * P:(k + 1) * P])
            pe.wait_ge(small_landed, SMALL)
            for j in range(4):
                mm = nc.tensor.transpose(prog.ps[:, 4, j * 2 * FT:(j + 1) * 2 * FT], craw[:, j, :],
                                         prog.ident[0:2 * FT, 0:2 * FT])
            mm.then_inc(cw_turned, 1)
            pe.wait_ge(turn.lo_done, turn.GROUPS)
            pe_columns_unit(prog, pe, w, 0, 0, None, acc_ready, 0)
            pe.wait_ge(cw_taken, 1)
            pe_columns_unit(prog, pe, w, 1, 1, None, acc_ready, 4)
            with pe.Fori(1, NU // 2) as pair:
                for slot in range(2):
                    u = pair * 2 + slot
                    pe.wait_ge(tap, u * 4 - 4)
                    pe_columns_unit(prog, pe, w, u, slot, None, acc_ready, 4 * slot)

        def banks(slot, part):
            return prog.ps[:, 4 * slot + 2 * part:4 * slot + 2 * part + 2, :].rearrange("p a b -> p (a b)")

        @block.scalar
        def _(act):
            norm.act(act, lambda e, t: e.wait_ge(x_landed[t // 2], 16))
            w.first_two(hi=act)
            act.wait_ge(small_landed, SMALL)
            turn.act(act)
            act.wait_ge(cw_turned, 1)
            nc.scalar.activation(CW[:].rearrange("p j f -> p (j f)"), prog.ps[:, 4, 0:8 * FT],
                                 ACT.Copy).then_inc(cw_taken, 1)
            act.wait_ge(cw_taken, 1)

            def unit(u, slot, first=False, more=True, visit=None):
                if not first:
                    act.wait_ge(a_done, u)
                act.wait_ge(acc_ready, u * 4 + 2)
                nc.scalar.activation(CG[:], banks(slot, 0), ACT.Identity, bias=CW[:, 3, bass.ds(u, 1)],
                                     scale=CW[:, 2, bass.ds(u, 1)]).then_inc(newest_tap, 1)
                act.wait_ge(acc_ready, u * 4 + 4)
                nc.scalar.activation(A[:, bass.ds(u, 1), :], banks(slot, 1), ACT.Identity,
                                     bias=CW[:, 3, bass.ds(u + FT, 1)],
                                     scale=CW[:, 2, bass.ds(u + FT, 1)]).then_inc(newest_tap, 1)
                if more:
                    w.split_hi(act, u + 2, slot, visit)
                act.wait_ge(tap, u * 4 + 2)
                nc.scalar.activation(CG[:], CG[:], ACT.Silu).then_inc(gate_done, 1)

            unit(0, 0, first=True, visit=1)
            unit(1, 1, visit=1)
            with act.Fori(1, NU // 2 - 1) as pair:
                for slot in range(2):
                    unit(pair * 2 + slot, slot, visit=pair + 1)
            for u in (NU - 2, NU - 1):
                unit(u, u % 2, more=False)

        @block.vector
        def _(dve):
            norm.dve(dve)
            w.first_two(lo=dve)
            dve.wait_ge(small_landed, SMALL)
            turn.dve(dve)
            dve.wait_ge(cw_taken, 1)

            def unit(u, slot, more=True):
                for part, (dst, f) in enumerate(((CG[:].unsqueeze(1), u), (A[:, bass.ds(u, 1), :], u + FT))):
                    dve.wait_ge(newest_tap, u * 2 + part + 1)
                    for back in (1, 2):
                        out = dst[:, :, back:]
                        nc.vector.scalar_tensor_tensor(out, banks(slot, part)[:, 0:SEQ - back].unsqueeze(1),
                                                       CW[:, 2 - back, bass.ds(f, 1)], out, ALU.mult,
                                                       ALU.add).then_inc(tap, 1)
                        dve.wait_ge(tap, u * 4 + 2 * part + back)
                if more:
                    w.split_lo(dve, u + 2, slot)
                dve.wait_ge(gate_done, u + 1)
                nc.vector.tensor_tensor(A[:, bass.ds(u, 1), :], A[:, bass.ds(u, 1), :], CG[:].unsqueeze(1),
                                        ALU.mult).then_inc(a_done, 1)

            with dve.Fori(0, NU // 2 - 1) as pair:
                for slot in range(2):
                    unit(pair * 2 + slot, slot)
            for u in (NU - 2, NU - 1):
                unit(u, u % 2, more=False)
    return A


def ffn_down(prog, a, A, x_src, out):
    nc = prog.nc
    kb = prog.B
    KU = 2
    NCOL = 512
    SIZE = KU * NCOL
    NU = FT // KU
    A_hi = prog.at("A_hi", [P, 2, KU, SEQ], 0, F32R)
    A_lo = prog.at("A_lo", [P, 2, KU, SEQ], 16, F32R)
    O = prog.at("O", [P, TT, D], 32)
    xin = [prog.at("xin", [P, D], 68), prog.at("xin", [P, D], 76)]
    fg = prog.at("fg", [P, D], 84)
    junk = prog.at("junk", [P, D], 92)
    stat = prog.at("stat", [P, 32], kb + 93)
    wv = a["ffn_w_down"].rearrange("(k p) n -> p k n", p=P)

    done = prog.sem("unit_done")
    halves = []

    def src(u, raw, half=None):
        raw = raw.rearrange("p (k n) -> p k n", k=KU)
        half = u // NU if half is None else half
        return [(raw, wv[:, bass.ds((u - half * NU) * KU, KU), half * NCOL:(half + 1) * NCOL])]

    w = Weights(prog, src, done, 1, size=SIZE)
    a_hi = prog.sem("a_hi_ready")
    a_lo = prog.sem("a_lo_ready")
    out_ready = prog.sem("out_ready")
    out_free = prog.sem("out_free")
    fg_landed = prog.sem("fg_landed")
    x_landed = [prog.sem("x_landed0"), prog.sem("x_landed1")]
    x_added = prog.sem("x_added")
    squared = prog.sem("squared")
    meaned = prog.sem("meaned")
    rooted = prog.sem("rooted")
    inverted = prog.sem("inverted")
    y_done = prog.sem("y_done")
    stored = prog.sem("stored")
    xv = x_src.rearrange("(t p) d -> p t d", p=P)
    ov = out.rearrange("(t p) d -> p t d", p=P)

    def tiles(u):
        i = u % NU
        return A[:, KU * i:KU * (i + 1), :]

    with nc.Block() as block:
        @block.sync
        def _(sp):
            w.first_two(load=sp)
            sp.dma_start(fg[:], a["final_norm"].rearrange("(o n) -> o n", o=1).to_broadcast([P, D])
                         ).then_inc(fg_landed, 16)
            for t in range(2):
                sp.dma_start(xin[t][:], xv[:, t, :]).then_inc(x_landed[t], 16)
            for u in range(2, 2 * NU):
                w.load(sp, u)
            for t in range(2, TT):
                sp.wait_ge(x_added, t - 1)
                sp.dma_start(xin[t % 2][:], xv[:, t, :]).then_inc(x_landed[t % 2], 16)
            for t in range(TT):
                sp.wait_ge(y_done, t + 1)
                sp.dma_start(ov[:, t, :], O[:, t, :]).then_inc(stored, 16)
            sp.wait_ge(stored, 16 * TT)

        @block.tensor
        def _(pe):
            def unit(u, slot, first=False, last=False, fresh=False):
                pe.wait_ge(w.lo_ready, u + 1)
                pe.wait_ge(a_lo, u + 1)
                for k in range(KU):
                    for t in range(TT):
                        if first and k == 0 and not fresh:
                            pe.wait_ge(out_free, t + 1)
                        tok = slice(t * P, (t + 1) * P)
                        col = slice(k * NCOL, (k + 1) * NCOL)
                        mm = three_products(nc, prog.ps[:, t, :], A_hi[:, slot, k, tok], A_lo[:, slot, k, tok],
                                            prog.w_hi[:, slot, col], prog.w_lo[:, slot, col],
                                            first and k == 0, last and k == KU - 1)
                        if last and k == KU - 1:
                            mm.then_inc(out_ready, 1)
                        elif k == KU - 1 and t == TT - 1:
                            mm.then_inc(done, 1)

            for half in range(2):
                u0 = half * NU
                unit(u0, u0 % 2, first=True, fresh=(half == 0))
                with pe.Fori(0, (NU - 3) // 2) as pair:
                    for j in range(2):
                        unit(pair * 2 + (u0 + 1 + j), (u0 + 1 + j) % 2)
                unit(u0 + NU - 2, (u0 + NU - 2) % 2)
                unit(u0 + NU - 1, (u0 + NU - 1) % 2, last=True)

        @block.scalar
        def _(act):
            def split(u):
                if u >= 2:
                    if u - 2 < NU - 1:
                        act.wait_ge(done, u - 1)
                    elif u - 2 == NU - 1:
                        act.wait_ge(out_ready, TT)
                    else:
                        act.wait_ge(done, u - 2)
                w.split_hi(act, u, reused=False)
                nc.scalar.activation(A_hi[:, u % 2, :, :], tiles(u), ACT.Copy).then_inc(a_hi, 1)

            def take(half, t):
                act.wait_ge(out_ready, half * TT + t + 1)
                nc.scalar.activation(O[:, t, half * NCOL:(half + 1) * NCOL], prog.ps[:, t, :],
                                     ACT.Copy).then_inc(out_free, 1)

            for u in range(NU + 1):
                split(u)
            for t in range(TT):
                take(0, t)
            for u in range(NU + 1, 2 * NU):
                split(u)
            for t in range(TT):
                take(1, t)
            for t in range(TT):
                act.wait_ge(x_added, t + 1)
                if t:
                    act.wait_ge(squared, t)
                nc.scalar.activation(junk[:], O[:, t, :], ACT.Square, accum_out=stat[:, t:t + 1]).then_inc(squared, 1)
            act.wait_ge(meaned, 1)
            nc.scalar.activation(stat[:, 8:16], stat[:, 16:24], ACT.Sqrt).then_inc(rooted, 1)

        @block.vector
        def _(dve):
            for u in range(2 * NU):
                w.split_lo(dve, u)
                dve.wait_ge(a_hi, u + 1)
                nc.vector.tensor_tensor(A_lo[:, u % 2, :, :], tiles(u), plane(A_hi[:, u % 2, :, :]),
                                        ALU.subtract).then_inc(a_lo, 1)
            for t in range(TT):
                dve.wait_ge(out_free, TT + t + 1)
                dve.wait_ge(x_landed[t % 2], 16 * (t // 2 + 1))
                nc.vector.tensor_tensor(O[:, t, :], O[:, t, :], xin[t % 2][:], ALU.add).then_inc(x_added, 1)
            dve.wait_ge(squared, TT)
            nc.vector.tensor_scalar(stat[:, 16:24], stat[:, 0:8], 1.0 / D, EPS, ALU.mult, ALU.add).then_inc(meaned, 1)
            dve.wait_ge(rooted, 1)
            nc.vector.reciprocal(stat[:, 24:32], stat[:, 8:16]).then_inc(inverted, 1)
            dve.wait_ge(inverted, 1)
            dve.wait_ge(fg_landed, 16)
            for t in range(TT):
                nc.vector.scalar_tensor_tensor(O[:, t, :], O[:, t, :], stat[:, 24 + t:25 + t], fg[:], ALU.mult,
                                               ALU.mult).then_inc(y_done, 1)


def build(nc, a, out):
    with ExitStack() as ctx:
        prog = Program(nc, ctx, a)
        x_mid = nc.dram_tensor("x_mid", (SEQ, D), F32).ap()
        make_constants(prog)
        prog.end_phase()
        O = prog.at("O", [P, TT, D], prog.B)
        for l in range(DEPTH):
            x_src = a["x"][0] if l == 0 else x_mid
            QKV, U, G = mixer_inputs(prog, l, x_src, a, None)
            prog.end_phase()
            attention(prog, l, QKV, G)
            prog.end_phase()

            def rows(t, k):
                src, k = (U, k) if k < 4 else (G, k - 4)
                return src[:, t, k * P:(k + 1) * P]

            output_rows(prog, a["w_out"][l], a["post_g"][l:l + 1, :], rows, x_src, x_mid, O)
            prog.end_phase()
        Q, K, V, DEC = gla_inputs(prog, a, x_mid)
        prog.end_phase()
        gla_core(prog, a, Q, K, V, DEC)
        prog.end_phase()
        output_rows(prog, a["gla_w_out"], None, lambda t, k: V[:, t, k * P:(k + 1) * P], x_mid, x_mid, O)
        prog.end_phase()
        A = ffn_up(prog, a, x_mid)
        prog.end_phase()
        ffn_down(prog, a, A, x_mid, out[0])


_USED = ["x", "w_in", "w_out", "pre_g", "post_g", "ln_a_g", "ln_a_b", "spatial_w", "spatial_b", "q_norm_g",
         "k_norm_g"]
_SECOND = ["norm1", "gla_w_in", "gla_w_alpha_up", "gla_b_alpha", "gla_out_norm", "gla_w_out", "norm2", "ffn_w_up",
           "ffn_conv_w", "ffn_conv_b", "ffn_w_down"]


def rope_tables():
    import numpy as np
    pos = np.arange(SEQ)
    row, col = (pos // 64).astype(np.float32), (pos % 64).astype(np.float32)
    inv = (np.float32(10000.0) ** (-np.arange(0, 32, 2, dtype=np.float32) / np.float32(32))).astype(np.float32)
    ar, ac = row[:, None] * inv, col[:, None] * inv
    cos = np.concatenate([np.cos(ar), np.cos(ar), np.cos(ac), np.cos(ac)], 1)
    sin = np.concatenate([-np.sin(ar), np.sin(ar), -np.sin(ac), np.sin(ac)], 1)
    return np.stack([cos, sin]).astype(np.float32)


def kernel(**inputs):
    import numpy as np
    import concourse.bacc as bacc
    from concourse import mybir as mb
    from concourse.bass_utils import run_bass_kernel_spmd as run

    nc = bacc.Bacc("TRN2", target_bir_lowering=False, num_devices=1)
    arrays, args = {}, {}
    given = {n: np.ascontiguousarray(inputs[n]) for n in _USED}
    given.update({n: np.ascontiguousarray(inputs[f"l0_{n}_2"]) for n in _SECOND})
    given["final_norm"] = np.ascontiguousarray(inputs["final_norm_2"])
    given["rope"] = rope_tables()
    for name, v in given.items():
        arrays[f"in_{name}"] = v
        args[name] = nc.dram_tensor(f"in_{name}", v.shape, mb.dt.from_np(v.dtype), kind="ExternalInput").ap()
    out = nc.dram_tensor("out", (1, SEQ, D), mb.dt.float32, kind="ExternalOutput").ap()
    build(nc, args, out)
    r = run(nc, [arrays], core_ids=[0])
    return r.results[0]["out"]
```

```python
from contextlib import ExitStack

import concourse.bass as bass
from concourse import mybir

ALU = mybir.AluOpType
ACT = mybir.ActivationFunctionType
AX = mybir.AxisListType
F32 = mybir.dt.float32
F32R = mybir.dt.float32r
U32 = mybir.dt.uint32

P = 128
SEQ = 1024
D = 1024
TT = SEQ // P
KT = D // P
UNIT = 256
DEPTH = 2
EPS = 1e-6
D_A = 512
H_A = 8
HD = 64
H_B = 8
KV = 2
COL_U, COL_VA, COL_GA, COL_Q, COL_KV, COL_GB = 0, 512, 1024, 1536, 2048, 2304
QKH = H_B + KV
GH = 4
DK = 128
DV = 256
RANK = 16
TAU = 16.0
CH = 64
FFN = 2816
FT = FFN // P

KB = 1024


def plane(ap):
    return ap.bitcast(F32)


class Program:

    def __init__(self, nc, ctx, consts):
        self.nc, self.ctx = nc, ctx
        self.base = nc.sbuf_base + (-nc.sbuf_base) % 64
        self.room = nc.sbuf_usable_end - self.base
        self.n = 0
        self.shift = 0
        self.phase_sems = []
        self.hT_hi = self.at("hT_hi", [P, KT, SEQ], 0, F32R)
        self.hT_lo = self.at("hT_lo", [P, KT, SEQ], 32, F32R)
        self.w_raw = self.at("w_raw", [P, 2, KT * UNIT], 64)
        self.w_hi = self.at("w_hi", [P, 2, KT * UNIT], 80, F32R)
        self.w_lo = self.at("w_lo", [P, 2, KT * UNIT], 96, F32R)
        self.B = 112
        self.ident = self.at("ident", [P, P], 206)
        self.eps = self.at("eps", [P, 1], 206.5)
        self.ps = ctx.enter_context(nc.psum_tensor("ps", [P, 8, 512], F32))

    def at(self, name, shape, kb, dt=F32):
        size = 4
        for s in shape[1:]:
            size *= s
        off = self.base + int(kb * KB)
        assert kb * KB + size <= self.room, (name, kb, size, self.room)
        self.n += 1
        return self.nc.alloc_sbuf_tensor_at(f"{name}_{self.n}", shape, dt, offset=off)

    def sem(self, name):
        self.n += 1
        sem = self.nc.alloc_semaphore(name=f"{name}_{self.n}")
        self.phase_sems.append(sem)
        return sem

    def end_phase(self):
        self.nc.clear_and_free_semaphores(self.phase_sems)
        self.nc.all_engine_barrier()
        self.phase_sems = []


class Stream:

    def __init__(self, src, size=KT * UNIT, pieces=1):
        self.src, self.size, self.pieces = src, size, pieces


def column_stream(w_rows, starts):
    wv = w_rows.rearrange("(k p) n -> p k n", p=P)

    def src(u, raw):
        return [(raw.rearrange("p (k n) -> p k n", k=KT), wv[:, :, starts[u]:starts[u] + UNIT])]

    return Stream(src)


class Weights:

    def __init__(self, prog, stream, units, done, done_at, follows):
        self.p, self.stream, self.units, self.shift = prog, stream, units, prog.shift
        self.done, self.done_at = done, done_at
        self.follows = follows
        prog.shift = (prog.shift + units) % 2
        self.landed = [prog.sem("w_landed0"), prog.sem("w_landed1")]
        self.hi_ready = prog.sem("w_hi_ready")
        self.lo_ready = prog.sem("w_lo_ready")

    def slot(self, u):
        return (u + self.shift) % 2

    def load(self, sp, u, slot=None):
        if not isinstance(u, int) or u >= 4:
            sp.wait_ge(self.lo_ready, u - 3)
        if isinstance(u, int):
            slot = self.slot(u)
        ahead = isinstance(u, int) and u >= self.units
        stream = self.follows if ahead else self.stream
        for dst, src in stream.src(u - self.units if ahead else u, self.p.w_raw[:, slot, 0:stream.size]):
            sp.dma_start(dst, src).then_inc(self.landed[slot], 16)

    def split_hi(self, act, u, slot=None, visit=None, wait_pe=True):
        if isinstance(u, int):
            slot, visit = self.slot(u), u // 2
        stream = self.follows if isinstance(u, int) and u >= self.units else self.stream
        act.wait_ge(self.landed[slot], (visit - 1) * (16 * self.stream.pieces) + 16 * stream.pieces)
        if wait_pe:
            act.wait_ge(self.done, self.done_at(u - 2))
        self.p.nc.scalar.activation(self.p.w_hi[:, slot, 0:stream.size], self.p.w_raw[:, slot, 0:stream.size],
                                    ACT.Copy).then_inc(self.hi_ready, 1)

    def split_lo(self, dve, u, slot=None, engine=None):
        engine = engine or self.p.nc.vector
        if isinstance(u, int):
            slot = self.slot(u)
        size = (self.follows if isinstance(u, int) and u >= self.units else self.stream).size
        dve.wait_ge(self.hi_ready, u - 1)
        engine.tensor_tensor(self.p.w_lo[:, slot, 0:size], self.p.w_raw[:, slot, 0:size],
                             plane(self.p.w_hi[:, slot, 0:size]), ALU.subtract).then_inc(self.lo_ready, 1)

    def ready(self, pe, u):
        pe.wait_ge(self.lo_ready, u - 1)


def three_products(nc, out, a_hi, a_lo, b_hi, b_lo, first, last):
    nc.tensor.matmul(out, a_hi, b_hi, start=first, stop=False)
    nc.tensor.matmul(out, a_hi, b_lo, start=False, stop=False)
    return nc.tensor.matmul(out, a_lo, b_hi, start=False, stop=last)


class Turn:

    GROUPS = 2 * KT

    def __init__(self, prog):
        self.p = prog
        self.turned = prog.sem("turned")
        self.hi_done = prog.sem("turn_hi_done")
        self.lo_done = prog.sem("turn_lo_done")

    def pe(self, pe, src):
        nc = self.p.nc
        for g in range(self.GROUPS):
            k, half = g // 2, g % 2
            if g >= 8:
                pe.wait_ge(self.lo_done, g - 7)
            for j in range(4):
                mm = nc.tensor.transpose(self.p.ps[:, g % 8, j * P:(j + 1) * P], src(half * 4 + j, k),
                                         self.p.ident[:])
            mm.then_inc(self.turned, 1)

    def act(self, act):
        for g in range(self.GROUPS):
            k, half = g // 2, g % 2
            act.wait_ge(self.turned, g + 1)
            self.p.nc.scalar.activation(self.p.hT_hi[:, k, half * 512:(half + 1) * 512], self.p.ps[:, g % 8, :],
                                        ACT.Copy).then_inc(self.hi_done, 1)

    def dve(self, dve):
        for g in range(self.GROUPS):
            k, half = g // 2, g % 2
            dve.wait_ge(self.hi_done, g + 1)
            self.p.nc.vector.tensor_tensor(self.p.hT_lo[:, k, half * 512:(half + 1) * 512], self.p.ps[:, g % 8, :],
                                           plane(self.p.hT_hi[:, k, half * 512:(half + 1) * 512]),
                                           ALU.subtract).then_inc(self.lo_done, 1)


class Prepare:

    def __init__(self, prog, X, gain_row, x_ready):
        kb = prog.B
        self.p, self.X, self.gain_row, self.x_ready = prog, X, gain_row, x_ready
        self.H = prog.at("H", [P, TT, D], kb + 40)
        self.junk = prog.at("junk", [P, D], kb + 76)
        self.gain = prog.at("gain", [P, D], kb + 88)
        self.stat = prog.at("pstat", [P, 3, TT], kb + 92)
        self.gain_landed = prog.sem("gain_landed")
        self.squared = prog.sem("x_squared")
        self.rooted = prog.sem("x_rooted")
        self.inverted = prog.sem("x_inverted")
        self.scaled = prog.sem("h_scaled")
        self.turned = prog.sem("h_turned")
        self.hi_done = prog.sem("h_hi_done")
        self.lo_done = prog.sem("h_lo_done")

    def load_gain(self, sp):
        sp.dma_start(self.gain[:], self.gain_row.to_broadcast([P, D])).then_inc(self.gain_landed, 16)

    def square(self, act, t):
        self.x_ready(act, t)
        if t:
            act.wait_ge(self.squared, t)
        self.p.nc.scalar.activation(self.junk[:], self.X[:, t, :], ACT.Square,
                                    accum_out=self.stat[:, 0, t:t + 1]).then_inc(self.squared, 1)

    def root(self, act, t):
        act.wait_ge(self.squared, t + 1)
        self.p.nc.scalar.activation(self.stat[:, 1, t:t + 1], self.stat[:, 0, t:t + 1], ACT.Sqrt,
                                    bias=self.p.eps[:], scale=1.0 / D).then_inc(self.rooted, 1)

    def scale(self, dve, t):
        nc = self.p.nc
        if t == 0:
            dve.wait_ge(self.gain_landed, 16)
        dve.wait_ge(self.rooted, t + 1)
        nc.vector.reciprocal(self.stat[:, 2, t:t + 1], self.stat[:, 1, t:t + 1]).then_inc(self.inverted, 1)
        dve.wait_ge(self.inverted, t + 1)
        nc.vector.scalar_tensor_tensor(self.H[:, t, :], self.X[:, t, :], self.stat[:, 2, t:t + 1], self.gain[:],
                                       ALU.mult, ALU.mult).then_inc(self.scaled, 1)

    def turn(self, pe, t):
        pe.wait_ge(self.scaled, t + 1)
        for kh in range(2):
            g = 2 * t + kh
            if g >= 4:
                pe.wait_ge(self.lo_done, g - 3)
            for j in range(4):
                k = 4 * kh + j
                mm = self.p.nc.tensor.transpose(self.p.ps[:, 4 + g % 4, j * P:(j + 1) * P],
                                                self.H[:, t, k * P:(k + 1) * P], self.p.ident[:])
            mm.then_inc(self.turned, 1)

    def place(self, hT, t, kh):
        return hT[:, 4 * kh:4 * kh + 4, t * P:(t + 1) * P]

    def bank(self, g):
        return self.p.ps[:, 4 + g % 4, :].rearrange("p (k n) -> p k n", k=4)

    def hi(self, act, t):
        for kh in range(2):
            g = 2 * t + kh
            act.wait_ge(self.turned, g + 1)
            self.p.nc.scalar.activation(self.place(self.p.hT_hi, t, kh), self.bank(g), ACT.Copy
                                        ).then_inc(self.hi_done, 1)

    def lo(self, dve, t):
        for kh in range(2):
            g = 2 * t + kh
            dve.wait_ge(self.hi_done, g + 1)
            self.p.nc.vector.tensor_tensor(self.place(self.p.hT_lo, t, kh), self.bank(g),
                                           plane(self.place(self.p.hT_hi, t, kh)), ALU.subtract
                                           ).then_inc(self.lo_done, 1)


def at_tile(step, engine, t):
    if 0 <= t < TT:
        step(engine, t)


def start(prog, a, follows, gain_row):
    nc = prog.nc
    X = prog.at("X", [P, TT, D], prog.B)
    x_landed = [prog.sem(f"x_landed{t}") for t in range(TT)]
    made = prog.sem("ident_made")
    eps_made = prog.sem("eps_made")

    def x_ready(act, t):
        act.wait_ge(x_landed[t], 16)

    prep = Prepare(prog, X, gain_row, x_ready)
    w_landed = [prog.sem("w_landed0"), prog.sem("w_landed1")]
    w_hi = prog.sem("w_hi_ready")
    w_lo = prog.sem("w_lo_ready")
    xv = a["x"][0].rearrange("(t p) d -> p t d", p=P)

    with nc.Block() as block:
        @block.sync
        def _(sp):
            for t in range(TT):
                sp.dma_start(X[:, t, :], xv[:, t, :]).then_inc(x_landed[t], 16)
                if t == 0:
                    prep.load_gain(sp)
            for u in range(2):
                for dst, src in follows.src(u, prog.w_raw[:, u, 0:follows.size]):
                    sp.dma_start(dst, src).then_inc(w_landed[u], 16)

        @block.gpsimd
        def _(pool):
            nc.gpsimd.memset(prog.ident[:], 0.0).then_inc(made, 1)
            nc.gpsimd.memset(prog.eps[:], EPS).then_inc(eps_made, 1)
            pool.wait_ge(made, 1)
            nc.gpsimd.affine_select(out=prog.ident[:], in_=prog.ident[:], compare_op=ALU.not_equal, fill=1.0,
                                    base=0, pattern=[[-1, P]], channel_multiplier=1).then_inc(made, 1)
            for u in range(2):
                pool.wait_ge(w_hi, u + 1)
                nc.gpsimd.tensor_tensor(prog.w_lo[:, u, :], prog.w_raw[:, u, :], plane(prog.w_hi[:, u, :]),
                                        ALU.subtract).then_inc(w_lo, 1)

        @block.tensor
        def _(pe):
            pe.wait_ge(made, 2)
            for t in range(TT):
                prep.turn(pe, t)

        @block.scalar
        def _(act):
            act.wait_ge(eps_made, 1)
            for i in range(TT + 3):
                at_tile(prep.square, act, i)
                at_tile(prep.root, act, i - 1)
                at_tile(prep.hi, act, i - 3)
                if TT - 1 <= i <= TT:
                    u = i - (TT - 1)
                    act.wait_ge(w_landed[u], 16)
                    nc.scalar.activation(prog.w_hi[:, u, :], prog.w_raw[:, u, :], ACT.Copy).then_inc(w_hi, 1)

        @block.vector
        def _(dve):
            for i in range(TT + 3):
                at_tile(prep.scale, dve, i - 1)
                at_tile(prep.lo, dve, i - 3)
    prog.end_phase()


def pe_rows_unit(prog, pe, w, unit, slot, acc_free, acc_ready, free_base, hT_hi, hT_lo, then=None):
    nc = prog.nc
    if not isinstance(unit, int) or unit >= 2:
        w.ready(pe, unit)
    for t in range(TT):
        if free_base is not None or t >= 4:
            pe.wait_ge(acc_free, (free_base if free_base is not None else 0) + t - 3)
        for k in range(KT):
            tok = slice(t * P, (t + 1) * P)
            col = slice(k * UNIT, (k + 1) * UNIT)
            mm = three_products(nc, prog.ps[:, t % 4, 0:UNIT], hT_hi[:, k, tok], hT_lo[:, k, tok],
                                prog.w_hi[:, slot, col], prog.w_lo[:, slot, col], k == 0, k == KT - 1)
            if k == KT - 1:
                mm.then_inc(acc_ready, 1)
        if then is not None:
            then(t)


MIXER_ORDER = [COL_KV, COL_Q, COL_Q + UNIT, COL_VA, COL_VA + UNIT, COL_U, COL_U + UNIT,
               COL_GA, COL_GA + UNIT, COL_GB, COL_GB + UNIT]


def mixer_inputs(prog, l, a, stream, follows):
    nc = prog.nc
    kb = prog.B
    QKV = prog.at("QKV", [P, TT, 768], kb)
    VA = prog.at("VA", [P, TT, D_A], kb + 24)
    U = prog.at("U", [P, TT, D_A], kb + 40)
    G = prog.at("G", [P, TT, D_A], kb + 56)
    s = kb + 72
    rope = prog.at("rope", [P, 2, TT, HD], s)
    ln_gb = prog.at("ln_gb", [P, 2, D_A], s + 4)
    qkg = prog.at("qkg", [P, 2, HD], s + 8)
    spb = prog.at("spb", [P, H_A], s + 8.75)
    hst = prog.at("hst", [P, 4, TT, QKH], s + 9)
    bn = prog.at("bn", [P, TT, 6], s + 10.25)
    mv = prog.at("mv", [P, TT, 2], s + 10.5)
    rstd = prog.at("rstd", [P, 2, TT], s + 10.75)
    sq = prog.at("sq", [P, QKH * HD], s + 11)
    rot = prog.at("rot", [P, QKH * HD], s + 13.5)
    wsT = prog.at("wsT", [P, H_A, P], s + 16)
    wsR = prog.at("wsR", [P, H_A, P], kb + 56)
    order = MIXER_ORDER
    NU = len(order)
    acc_ready = prog.sem("acc_ready")
    w = Weights(prog, stream, NU, acc_ready, lambda u: (u + 1) * TT, follows)
    small_landed = prog.sem("small_landed")
    acc_free = prog.sem("acc_free")
    ws_turned = prog.sem("ws_turned")
    ws_taken = prog.sem("ws_taken")
    head_sq = prog.sem("head_sq")
    head_sum = prog.sem("head_sum")
    head_root = prog.sem("head_root")
    head_inv = prog.sem("head_inv")
    rope_step = prog.sem("rope_step")
    ln_stat = prog.sem("ln_stat")
    ln_root = prog.sem("ln_root")
    ln_step = prog.sem("ln_step")
    ln_scaled = prog.sem("ln_scaled")
    ln_done = prog.sem("ln_done")
    ga_used = prog.sem("ga_used")
    z_ready = prog.sem("z_ready")
    ya_done = prog.sem("ya_done")

    with nc.Block() as block:
        @block.sync
        def _(sp):
            w.load(sp, 2)
            w.load(sp, 3)
            sp.dma_start(wsR[:], a["spatial_w"][l].rearrange("h i j -> i h j")).then_inc(small_landed, 16)
            sp.dma_start(spb[:], a["spatial_b"][l].rearrange("h i -> i h"),
                         allow_slow_non_contiguous=True).then_inc(small_landed, 16)
            sp.dma_start(rope[:], a["rope"].rearrange("c (t p) d -> p c t d", p=P)).then_inc(small_landed, 16)
            sp.dma_start(ln_gb[:, 0, :], a["ln_a_g"][l:l + 1, :].to_broadcast([P, D_A])).then_inc(small_landed, 16)
            sp.dma_start(ln_gb[:, 1, :], a["ln_a_b"][l:l + 1, :].to_broadcast([P, D_A])).then_inc(small_landed, 16)
            sp.dma_start(qkg[:, 0, :], a["q_norm_g"][l:l + 1, :].to_broadcast([P, HD])).then_inc(small_landed, 16)
            sp.dma_start(qkg[:, 1, :], a["k_norm_g"][l:l + 1, :].to_broadcast([P, HD])).then_inc(small_landed, 16)
            for u in range(4, NU + 2):
                w.load(sp, u)

        SMALL = 7 * 16

        @block.tensor
        def _(pe):
            pe_rows_unit(prog, pe, w, 0, w.slot(0), acc_free, acc_ready, None, prog.hT_hi, prog.hT_lo)
            pe.wait_ge(small_landed, SMALL)
            for h in range(H_A):
                mm = nc.tensor.transpose(prog.ps[:, 4 + h // 4, h % 4 * P:(h % 4 + 1) * P], wsR[:, h, :],
                                         prog.ident[:])
            mm.then_inc(ws_turned, 1)
            pe_rows_unit(prog, pe, w, 1, w.slot(1), acc_free, acc_ready, TT, prog.hT_hi, prog.hT_lo)
            pe_rows_unit(prog, pe, w, 2, w.slot(2), acc_free, acc_ready, 2 * TT, prog.hT_hi, prog.hT_lo)
            with pe.Fori(1, (NU - 1) // 2) as pair:
                for j in range(2):
                    unit = pair * 2 + 1 + j
                    pe_rows_unit(prog, pe, w, unit, w.slot(1 + j), acc_free, acc_ready, unit * TT,
                                 prog.hT_hi, prog.hT_lo)
            pe.wait_ge(ln_done, TT)
            pe.wait_ge(ws_taken, 2)
            for h in range(H_A):
                if h >= 4:
                    pe.wait_ge(ya_done, h - 3)
                nc.tensor.matmul(prog.ps[:, 4 + h % 4, :].rearrange("p (c d) -> p c d", c=TT), wsT[:, h, :],
                                 VA[:, :, h * HD:(h + 1) * HD], start=True, stop=True).then_inc(z_ready, 1)

        @block.scalar
        def _(act):
            for u, col in enumerate(order):
                for t in range(TT):
                    act.wait_ge(acc_ready, u * TT + t + 1)
                    c0 = order[u] % 512
                    if col == COL_KV:
                        dst, f = QKV[:, t, 512:768], ACT.Copy
                    elif COL_Q <= col < COL_KV:
                        dst, f = QKV[:, t, c0:c0 + UNIT], ACT.Copy
                    elif COL_VA <= col < COL_GA:
                        dst, f = VA[:, t, c0:c0 + UNIT], ACT.Copy
                    elif col < COL_VA:
                        dst, f = U[:, t, c0:c0 + UNIT], ACT.Copy
                    else:
                        dst, f = G[:, t, (u - 1) % 2 * UNIT:((u - 1) % 2 + 1) * UNIT], ACT.Silu
                        if col >= COL_GB:
                            act.wait_ge(ga_used, t + 1)
                    nc.scalar.activation(dst, prog.ps[:, t % 4, 0:UNIT], f).then_inc(acc_free, 1)
                w.split_hi(act, u + 2)
                if u == 0:
                    act.wait_ge(ws_turned, 1)
                    for b in range(2):
                        nc.scalar.copy(wsT[:, 4 * b:4 * b + 4, :], prog.ps[:, 4 + b, :].rearrange("p (h i) -> p h i", h=4)
                                       ).then_inc(ws_taken, 1)
                if u == 3:
                    act.wait_ge(head_sum, 2)
                    nc.scalar.activation(hst[:, 2, :, :], hst[:, 1, :, :], ACT.Sqrt).then_inc(head_root, 1)
                if u == 6:
                    act.wait_ge(ln_stat, 3)
                    nc.scalar.activation(rstd[:, 0, :], rstd[:, 1, :], ACT.Sqrt).then_inc(ln_root, 1)

        @block.vector
        def _(dve):
            dve.wait_ge(small_landed, SMALL)
            for u in range(NU):
                if u == 3:
                    for t in range(TT):
                        if t == 0:
                            dve.wait_ge(acc_free, 3 * TT)
                        if t:
                            dve.wait_ge(head_inv, t)
                        nc.vector.tensor_tensor(sq[:], QKV[:, t, 0:QKH * HD], QKV[:, t, 0:QKH * HD],
                                                ALU.mult).then_inc(head_sq, 1)
                        dve.wait_ge(head_sq, t + 1)
                        nc.vector.tensor_reduce(hst[:, 0, t, :], sq[:].rearrange("p (h d) -> p h d", d=HD), AX.X,
                                                ALU.add).then_inc(head_inv, 1)
                    dve.wait_ge(head_inv, TT)
                    nc.vector.tensor_scalar(hst[:, 1, :, :], hst[:, 0, :, :], 1.0 / HD, EPS, ALU.mult,
                                            ALU.add).then_inc(head_sum, 2)
                if u == 4:
                    dve.wait_ge(head_root, 1)
                    nc.vector.reciprocal(hst[:, 3, :, :], hst[:, 2, :, :]).then_inc(head_inv, 1)
                if u == 6:
                    dve.wait_ge(acc_free, 5 * TT)
                    for t in range(TT):
                        nc.vector.bn_stats(bn[:, t, :], VA[:, t, :]).then_inc(ln_step, 1)
                    for t in range(TT):
                        dve.wait_ge(ln_step, t + 1)
                        nc.vector.bn_aggr(mv[:, t, :], bn[:, t, :]).then_inc(ln_step, 1)
                    dve.wait_ge(ln_step, 2 * TT)
                    nc.vector.tensor_scalar(rstd[:, 1, :], mv[:, :, 1], 1.0, EPS, ALU.mult,
                                            ALU.add).then_inc(ln_stat, 3)
                if u == 8:
                    dve.wait_ge(ln_root, 1)
                    nc.vector.reciprocal(rstd[:, 1, :], rstd[:, 0, :]).then_inc(ln_step, 1)
                    dve.wait_ge(ln_step, 2 * TT + 1)
                    for t in range(TT):
                        nc.vector.tensor_scalar(VA[:, t, :], VA[:, t, :], mv[:, t, 0:1], rstd[:, 1, t:t + 1],
                                                ALU.subtract, ALU.mult).then_inc(ln_scaled, 1)
                if u < NU - 1:
                    w.split_lo(dve, u + 2)
            dve.wait_ge(ga_used, TT)
            for h in range(H_A):
                dve.wait_ge(z_ready, h + 1)
                nc.vector.scalar_tensor_tensor(U[:, :, h * HD:(h + 1) * HD],
                                               prog.ps[:, 4 + h % 4, :].rearrange("p (c d) -> p c d", c=TT),
                                               spb[:, h:h + 1], U[:, :, h * HD:(h + 1) * HD], ALU.add,
                                               ALU.mult).then_inc(ya_done, 1)

        @block.gpsimd
        def _(pool):
            n = 0
            pool.wait_ge(small_landed, SMALL)
            pool.wait_ge(head_inv, TT + 1)

            def step(ins):
                nonlocal n
                n += 1
                ins.then_inc(rope_step, 1)

            def after():
                pool.wait_ge(rope_step, n)

            for t in range(TT):
                qk = QKV[:, t, 0:QKH * HD]
                heads = qk.rearrange("p (h d) -> p h d", d=HD)
                rh = rot[:].rearrange("p (h d) -> p h d", d=HD)
                sgn = rope[:, 1, t, :].rearrange("p (a b e) -> p a b e", a=2, b=2)
                step(nc.gpsimd.tensor_tensor(heads, heads, hst[:, 3, t, :].unsqueeze(2).to_broadcast([P, QKH, HD]),
                                             ALU.mult))
                after()
                step(nc.gpsimd.tensor_tensor(heads[:, 0:H_B, :], heads[:, 0:H_B, :],
                                             qkg[:, 0, :].unsqueeze(1).to_broadcast([P, H_B, HD]), ALU.mult))
                step(nc.gpsimd.tensor_tensor(heads[:, H_B:, :], heads[:, H_B:, :],
                                             qkg[:, 1, :].unsqueeze(1).to_broadcast([P, KV, HD]), ALU.mult))
                after()
                for x in range(2):
                    for b in range(2):
                        h4 = rh[:, :, 32 * x + 16 * b:32 * x + 16 * b + 16]
                        o4 = heads[:, :, 32 * x + 16 * (1 - b):32 * x + 16 * (1 - b) + 16]
                        sn = sgn[:, x, b, :].unsqueeze(1).to_broadcast([P, QKH, 16])
                        step(nc.gpsimd.tensor_tensor(h4, o4, sn, ALU.mult))
                after()
                step(nc.gpsimd.tensor_tensor(heads, heads, rope[:, 0, t, :].unsqueeze(1).to_broadcast([P, QKH, HD]),
                                             ALU.mult))
                after()
                step(nc.gpsimd.tensor_tensor(qk, qk, rot[:], ALU.add))
                after()
            for t in range(TT):
                pool.wait_ge(ln_scaled, t + 1)
                step(nc.gpsimd.tensor_tensor(VA[:, t, :], VA[:, t, :], ln_gb[:, 0, :], ALU.mult))
                after()
                nc.gpsimd.tensor_tensor(VA[:, t, :], VA[:, t, :], ln_gb[:, 1, :], ALU.add).then_inc(ln_done, 1)
            pool.wait_ge(acc_free, 9 * TT)
            for t in range(TT):
                nc.gpsimd.tensor_tensor(U[:, t, :], U[:, t, :], G[:, t, :], ALU.mult).then_inc(ga_used, 1)
            w.split_lo(pool, NU + 1, engine=nc.gpsimd)
    prog.end_phase()
    return QKV, U, G


def attention(prog, l, QKV, G):
    nc = prog.nc
    QT_hi = prog.at("QT_hi", [P, 2, SEQ], 0, F32R)
    QT_lo = prog.at("QT_lo", [P, 2, SEQ], 8, F32R)
    KT_st = prog.at("KT_st", [P, KV, SEQ], 16, F32R)
    KT_hi = prog.at("KT_hi", [P, SEQ], 24, F32R)
    PR = prog.at("PR", [P, 2, SEQ], 32)
    PT = prog.at("PT", [P, 2, TT, P], 40)
    TWICE = prog.at("TWICE", [P, 2, TT, 2 * HD], 50)
    nmx = prog.at("nmx", [P, 64], 48.25)
    sm = prog.at("sm", [P, 64], 48.5)
    inv = prog.at("inv", [P, 64], 48.75)
    NT = H_B * TT
    SCALE = HD ** -0.5

    doubled_first = prog.sem("doubled_first")
    doubled = prog.sem("doubled")
    turned = prog.sem("turned")
    k_top = prog.sem("k_top")
    hi_done = prog.sem("hi_done")
    lo_done = prog.sem("lo_done")
    s_ready = prog.sem("s_ready")
    max_done = prog.sem("max_done")
    exp_done = prog.sem("exp_done")
    p_turned = prog.sem("p_turned")
    pt_a = prog.sem("pt_taken_a")
    pt_b = prog.sem("pt_taken_b")
    o_ready = prog.sem("o_ready")
    inv_done = prog.sem("inv_done")
    o_done = prog.sem("o_done")

    def turn_bank(n):
        return 6 + n % 2 if n < 2 * KV + 2 else 6

    with nc.Block() as block:
        @block.tensor
        def _(pe):
            def turn_head(item, half):
                n = 2 * item + half
                if item <= KV:
                    pe.wait_ge(doubled_first, item + 1)
                else:
                    pe.wait_ge(doubled, item - KV)
                if n >= 2:
                    pe.wait_ge(lo_done, n - 1 if item <= KV else n)
                for j in range(4):
                    mm = nc.tensor.transpose(prog.ps[:, turn_bank(n), j * P:(j + 1) * P],
                                             TWICE[:, item % 2, half * 4 + j, :], prog.ident[:])
                mm.then_inc(turned, 1)

            def scores(n):
                head, t = n // TT, n % TT
                if t == 0:
                    pe.wait_ge(lo_done, 2 * (KV + head) + 2)
                    pe.wait_ge(k_top, 2 * KV)
                if n >= 2:
                    pe.wait_ge(exp_done, n - 1)
                for half in range(2):
                    keys = KT_st[:, head // (H_B // KV), half * 512:(half + 1) * 512]
                    out = prog.ps[:, 2 * (n % 2) + half, :]
                    nc.tensor.matmul(out, QT_hi[:, head % 2, t * P:(t + 1) * P], keys, start=True, stop=False)
                    mm = nc.tensor.matmul(out, QT_lo[:, head % 2, t * P:(t + 1) * P], keys, start=False, stop=True)
                mm.then_inc(s_ready, 1)

            def turn_p(n):
                pe.wait_ge(exp_done, n + 1)
                for half in range(2):
                    if n >= 1:
                        pe.wait_ge(pt_a if half == 0 else pt_b, n)
                    for j in range(4):
                        k = half * 4 + j
                        mm = nc.tensor.transpose(prog.ps[:, 4 + half, j * P:(j + 1) * P],
                                                 PR[:, n % 2, k * P:(k + 1) * P], prog.ident[:])
                    mm.then_inc(p_turned, 1)

            def values(n):
                head = n // TT
                g = head // (H_B // KV)
                if n >= 1:
                    pe.wait_ge(o_done, n)
                pe.wait_ge(pt_a, n + 1)
                pe.wait_ge(pt_b, n + 1)
                for k in range(TT):
                    mm = nc.tensor.matmul(prog.ps[:, 7, 0:HD], PT[:, n % 2, k, :],
                                          QKV[:, k, 640 + g * HD:640 + (g + 1) * HD], start=(k == 0),
                                          stop=(k == TT - 1))
                mm.then_inc(o_ready, 1)

            for item in range(KV + 1):
                turn_head(item, 0)
                turn_head(item, 1)
            for n in range(NT + 2):
                if n < NT:
                    scores(n)
                if 1 <= n <= NT:
                    turn_p(n - 1)
                if n >= 2:
                    values(n - 2)
                if n % TT in (2, 4) and n // TT + 1 < H_B:
                    turn_head(KV + n // TT + 1, n % TT // 4)

        @block.scalar
        def _(act):
            for i in range(2 * KV):
                act.wait_ge(turned, i + 1)
                cols = slice(i % 2 * 512, (i % 2 + 1) * 512)
                nc.scalar.activation(KT_st[0:HD, i // 2, cols], prog.ps[0:HD, turn_bank(i), :],
                                     ACT.Copy).then_inc(k_top, 1)
                if i >= 2:
                    act.wait_ge(lo_done, i - 1)
                nc.scalar.activation(KT_hi[HD:P, cols], prog.ps[HD:P, turn_bank(i), :], ACT.Copy).then_inc(hi_done, 1)

            def q_split(head, half):
                act.wait_ge(turned, 2 * (KV + head) + half + 1)
                nc.scalar.activation(QT_hi[:, head % 2, half * 512:(half + 1) * 512],
                                     prog.ps[:, turn_bank(2 * (KV + head) + half), :], ACT.Copy, scale=SCALE).then_inc(hi_done, 1)

            q_split(0, 0)
            q_split(0, 1)
            for n in range(NT + 1):
                if n < NT:
                    act.wait_ge(max_done, n + 1)
                    if n >= 2:
                        act.wait_ge(p_turned, 2 * n - 2)
                    nc.scalar.activation(PR[:, n % 2, :].rearrange("p (a b) -> p a b", a=2),
                                         prog.ps[:, 2 * (n % 2):2 * (n % 2) + 2, :], ACT.Exp,
                                         bias=nmx[:, n:n + 1],
                                         accum_out=sm[:, n:n + 1]).then_inc(exp_done, 1)
                if n >= 1:
                    m = n - 1
                    act.wait_ge(p_turned, 2 * m + 1)
                    if m >= 2:
                        act.wait_ge(o_ready, m - 1)
                    nc.scalar.activation(PT[:, m % 2, 0:4, :], prog.ps[:, 4, :].rearrange("p (a b) -> p a b", a=4),
                                         ACT.Copy).then_inc(pt_a, 1)
                if n % TT in (3, 5) and n // TT + 1 < H_B:
                    q_split(n // TT + 1, n % TT // 4)

        @block.gpsimd
        def _(pool):
            for item in range(KV + 1, KV + H_B):
                head = item - KV
                pool.wait_ge(turned, 2 * item - 2)
                src = QKV[:, :, head * HD:(head + 1) * HD]
                nc.gpsimd.tensor_copy(TWICE[:, item % 2, :, 0:HD], src)
                nc.gpsimd.tensor_copy(TWICE[:, item % 2, :, HD:], src).then_inc(doubled, 1)

        @block.vector
        def _(dve):
            def double(item):
                head = (H_B + item) if item < KV else 0
                for side in range(2):
                    ins = nc.vector.tensor_copy(TWICE[:, item % 2, :, side * HD:(side + 1) * HD],
                                                QKV[:, :, head * HD:(head + 1) * HD])
                ins.then_inc(doubled_first, 1)

            for item in range(KV):
                double(item)
            for i in range(2 * KV):
                if i == 2:
                    dve.wait_ge(turned, 2)
                    double(KV)
                dve.wait_ge(hi_done, i + 1)
                nc.vector.tensor_tensor(KT_st[HD:P, i // 2, i % 2 * 512:(i % 2 + 1) * 512],
                                        prog.ps[HD:P, turn_bank(i), :],
                                        plane(KT_hi[HD:P, i % 2 * 512:(i % 2 + 1) * 512]),
                                        ALU.subtract).then_inc(lo_done, 1)

            def q_split(head, half):
                dve.wait_ge(hi_done, 2 * (KV + head) + half + 1)
                cols = slice(half * 512, (half + 1) * 512)
                nc.vector.scalar_tensor_tensor(QT_lo[:, head % 2, cols],
                                               prog.ps[:, turn_bank(2 * (KV + head) + half), :], SCALE, plane(QT_hi[:, head % 2, cols]), ALU.mult,
                                               ALU.subtract).then_inc(lo_done, 1)

            q_split(0, 0)
            q_split(0, 1)
            for n in range(NT + 2):
                if n < NT:
                    dve.wait_ge(s_ready, n + 1)
                    nc.vector.tensor_reduce(nmx[:, n:n + 1], prog.ps[:, 2 * (n % 2):2 * (n % 2) + 2, :], AX.XY,
                                            ALU.max, negate=True).then_inc(max_done, 1)
                if 1 <= n <= NT:
                    m = n - 1
                    dve.wait_ge(p_turned, 2 * m + 2)
                    if m >= 2:
                        dve.wait_ge(o_ready, m - 1)
                    nc.vector.tensor_copy(PT[:, m % 2, 4:8, :], prog.ps[:, 5, :].rearrange("p (a b) -> p a b", a=4)
                                          ).then_inc(pt_b, 1)
                    dve.wait_ge(exp_done, m + 1)
                    nc.vector.reciprocal(inv[:, m:m + 1], sm[:, m:m + 1]).then_inc(inv_done, 1)
                if n >= 2:
                    m = n - 2
                    head, t = m // TT, m % TT
                    dve.wait_ge(inv_done, m + 1)
                    dve.wait_ge(o_ready, m + 1)
                    dst = G[:, t, head * HD:(head + 1) * HD]
                    nc.vector.scalar_tensor_tensor(dst, prog.ps[:, 7, 0:HD], inv[:, m:m + 1], dst, ALU.mult,
                                                   ALU.mult).then_inc(o_done, 1)
                if n % TT in (3, 5) and n // TT + 1 < H_B:
                    q_split(n // TT + 1, n % TT // 4)
    prog.end_phase()


def output_rows(prog, stream, follows, post_g, next_gain, src, x_src, x_dst):
    nc = prog.nc
    kb = prog.B
    NU = D // UNIT
    O = prog.at("O", [P, TT, D], kb)
    pg = prog.at("pg", [P, D], kb + 72)
    ojunk = prog.at("ojunk", [P, UNIT], kb + 36)
    xin = prog.at("xin", [P, 2, D], kb + 80)
    ostat = prog.at("ostat", [P, TT, NU], kb + 92.5)
    osum = prog.at("osum", [P, 3, TT], kb + 93)

    acc_ready = prog.sem("acc_ready")
    w = Weights(prog, stream, NU, acc_ready, lambda u: (u + 1) * TT, follows)
    turn = Turn(prog)
    acc_free = prog.sem("acc_free")
    pg_landed = prog.sem("pg_landed")
    x_landed = [prog.sem("x_landed0"), prog.sem("x_landed1")]
    o_squared = prog.sem("o_squared")
    o_summed = prog.sem("o_summed")
    o_rooted = prog.sem("o_rooted")
    o_inverted = prog.sem("o_inverted")
    normed = prog.sem("normed")
    x_done = prog.sem("x_done")
    stored = prog.sem("stored")
    xv = x_src.rearrange("(t p) d -> p t d", p=P)
    ov = x_dst.rearrange("(t p) d -> p t d", p=P)
    prep = Prepare(prog, O, next_gain, lambda e, t: e.wait_ge(x_done, t + 1))
    LAG = 6

    with nc.Block() as block:
        @block.sync
        def _(sp):
            w.load(sp, 2)
            w.load(sp, 3)
            for u in range(4, NU + 2):
                w.load(sp, u)
            sp.wait_ge(turn.lo_done, turn.GROUPS)
            prep.load_gain(sp)
            if post_g is not None:
                sp.dma_start(pg[:], post_g.to_broadcast([P, D])).then_inc(pg_landed, 16)
            for t in range(2):
                sp.dma_start(xin[:, t, :], xv[:, t, :]).then_inc(x_landed[t], 16)
            for t in range(TT):
                sp.wait_ge(x_done, t + 1)
                if t + 2 < TT:
                    sp.dma_start(xin[:, t % 2, :], xv[:, t + 2, :]).then_inc(x_landed[t % 2], 16)
                sp.dma_start(ov[:, t, :], O[:, t, :]).then_inc(stored, 16)
            sp.wait_ge(stored, 16 * TT)

        @block.tensor
        def _(pe):
            turn.pe(pe, src)
            pe.wait_ge(turn.lo_done, turn.GROUPS)
            for u in range(NU):
                last = u == NU - 1
                pe_rows_unit(prog, pe, w, u, w.slot(u), acc_free, acc_ready, u * TT if u else None,
                             prog.hT_hi, prog.hT_lo,
                             then=(lambda t: at_tile(prep.turn, pe, t - LAG)) if last else None)
            for t in range(TT - LAG, TT):
                prep.turn(pe, t)

        @block.scalar
        def _(act):
            def take(u, t):
                n = u * TT + t
                act.wait_ge(acc_ready, n + 1)
                if post_g is not None:
                    if n:
                        act.wait_ge(o_squared, n)
                    nc.scalar.activation(ojunk[:], prog.ps[:, t % 4, 0:UNIT], ACT.Square,
                                         accum_out=ostat[:, t, u:u + 1]).then_inc(o_squared, 1)
                nc.scalar.activation(O[:, t, u * UNIT:(u + 1) * UNIT], prog.ps[:, t % 4, 0:UNIT],
                                     ACT.Copy).then_inc(acc_free, 1)

            def o_root(act, t):
                act.wait_ge(o_summed, t + 1)
                nc.scalar.activation(osum[:, 1, t:t + 1], osum[:, 0, t:t + 1], ACT.Sqrt, bias=prog.eps[:],
                                     scale=1.0 / D).then_inc(o_rooted, 1)

            turn.act(act)
            for u in range(NU - 1):
                for t in range(TT):
                    take(u, t)
                w.split_hi(act, u + 2)
            for i in range(TT + LAG):
                if i < TT:
                    take(NU - 1, i)
                if post_g is not None:
                    at_tile(o_root, act, i - 1)
                at_tile(prep.square, act, i - 3)
                at_tile(prep.root, act, i - 3)
                at_tile(prep.hi, act, i - LAG)
                if i == TT + 1:
                    w.split_hi(act, NU + 1)

        @block.vector
        def _(dve):
            def o_sum(dve, t):
                dve.wait_ge(acc_free, (NU - 1) * TT + t + 1)
                nc.vector.tensor_reduce(osum[:, 0, t:t + 1], ostat[:, t, :], AX.X, ALU.add).then_inc(o_summed, 1)

            def o_scale(dve, t):
                dve.wait_ge(o_rooted, t + 1)
                nc.vector.reciprocal(osum[:, 2, t:t + 1], osum[:, 1, t:t + 1]).then_inc(o_inverted, 1)
                dve.wait_ge(o_inverted, t + 1)
                if t == 0:
                    dve.wait_ge(pg_landed, 16)
                nc.vector.scalar_tensor_tensor(O[:, t, :], O[:, t, :], osum[:, 2, t:t + 1], pg[:], ALU.mult,
                                               ALU.mult).then_inc(normed, 1)

            turn.dve(dve)
            for u in range(NU - 1):
                w.split_lo(dve, u + 2)
            for i in range(TT + LAG):
                if post_g is not None:
                    at_tile(o_sum, dve, i)
                    at_tile(o_scale, dve, i - 1)
                at_tile(prep.scale, dve, i - 3)
                at_tile(prep.lo, dve, i - LAG)

        @block.gpsimd
        def _(pool):
            for t in range(TT):
                if post_g is not None:
                    pool.wait_ge(normed, t + 1)
                else:
                    pool.wait_ge(acc_free, (NU - 1) * TT + t + 1)
                pool.wait_ge(x_landed[t % 2], 16 * (t // 2 + 1))
                nc.gpsimd.tensor_tensor(O[:, t, :], O[:, t, :], xin[:, t % 2, :], ALU.add).then_inc(x_done, 1)
            w.split_lo(pool, NU + 1, engine=nc.gpsimd)
    prog.end_phase()


def pe_columns_unit(prog, pe, w, unit, slot, waits, acc_ready, bank):
    nc = prog.nc
    if not isinstance(unit, int) or unit >= 2:
        w.ready(pe, unit)
    for i in range(4):
        j, half = i // 2, i % 2
        if waits is not None:
            waits(i)
        for k in range(KT):
            wc = slice(k * UNIT + j * P, k * UNIT + (j + 1) * P)
            tok = slice(half * 512, (half + 1) * 512)
            mm = three_products(nc, prog.ps[:, bank + i, :], prog.w_hi[:, slot, wc], prog.w_lo[:, slot, wc],
                                prog.hT_hi[:, k, tok], prog.hT_lo[:, k, tok], k == 0, k == KT - 1)
        mm.then_inc(acc_ready, 1)


GLA_ORDER = [1024 + UNIT * i for i in range(4)] + [0, UNIT, 512, 512 + UNIT]


def gla_inputs(prog, a, stream, follows):
    nc = prog.nc
    kb = prog.B
    Q = prog.at("Qd", [P, GH, SEQ], kb)
    K = prog.at("Kd", [P, GH, SEQ], kb + 16)
    B = prog.at("Bc", [P, GH, SEQ], kb + 32)
    V = prog.at("V", [P, TT, GH * DV], kb + 48)
    wa_raw = prog.at("wa_raw", [P, KT, P], kb + 32)
    wa_hi = prog.at("wa_hi", [P, KT, P], kb + 36, F32R)
    wa_lo = prog.at("wa_lo", [P, KT, P], kb + 40, F32R)
    AL = prog.at("AL", [RANK, SEQ], kb + 44)
    tmp = prog.at("tmp", [P, 2, 512], kb + 80)
    keep = prog.at("keep", [P, SEQ], kb + 84)
    wau = prog.at("wau", [RANK, GH * DK], kb + 88)
    ba = prog.at("ba", [P, GH], kb + 90)
    DEC = prog.at("DEC", [P, GH, SEQ // CH], kb + 92)
    NU = len(GLA_ORDER)
    ROWS = 4
    wv = a["gla_w_in"].rearrange("(k p) n -> p k n", p=P)

    acc_ready = prog.sem("acc_ready")

    def sums(u):
        return TT * (u + 1) if u < ROWS else TT * ROWS + 4 * (u + 1 - ROWS)

    w = Weights(prog, stream, NU, acc_ready, sums, follows)
    small_landed = prog.sem("small_landed")
    acc_free = prog.sem("acc_free")
    wa_zero = prog.sem("wa_zero")
    wa_landed = prog.sem("wa_landed")
    wa_split = prog.sem("wa_split")
    wa_done = prog.sem("wa_done")
    al_ready = prog.sem("al_ready")
    al_taken = prog.sem("al_taken")
    z_ready = prog.sem("z_ready")
    z_abs = prog.sem("z_abs")
    z_exp = prog.sem("z_exp")
    z_min = prog.sem("z_min")
    z_log = prog.sem("z_log")
    keep_made = prog.sem("keep_made")
    ls_done = prog.sem("ls_done")
    b_done = prog.sem("b_done")
    e_done = prog.sem("e_done")
    Bv = B[:].rearrange("p h (c s) -> p h c s", s=CH)

    with nc.Block() as block:
        @block.sync
        def _(sp):
            sp.dma_start(wau[:], a["gla_w_alpha_up"]).then_inc(small_landed, 16)
            sp.dma_start(ba[:], a["gla_b_alpha"].rearrange("(h p) -> p h", p=P),
                         allow_slow_non_contiguous=True).then_inc(small_landed, 16)
            sp.wait_ge(wa_zero, 1)
            sp.dma_start(wa_raw[:, :, 0:RANK], wv[:, :, 3072:3072 + RANK]).then_inc(wa_landed, 16)
            for u in range(2, NU + 2):
                w.load(sp, u)

        SMALL = 2 * 16

        @block.gpsimd
        def _(pool):
            nc.gpsimd.memset(wa_raw[:], 0.0).then_inc(wa_zero, 1)
            nc.gpsimd.memset(keep[:], 1.0).then_inc(keep_made, 1)
            pool.wait_ge(keep_made, 1)
            nc.gpsimd.memset(keep[:].rearrange("p (c s) -> p c s", s=CH)[:, :, 0], 0.0).then_inc(keep_made, 1)

        @block.tensor
        def _(pe):
            pe.wait_ge(wa_split, 2)
            for half in range(2):
                tok = slice(half * 512, (half + 1) * 512)
                for k in range(KT):
                    mm = three_products(nc, prog.ps[:, 4 + half, :], wa_hi[:, k, :], wa_lo[:, k, :],
                                        prog.hT_hi[:, k, tok], prog.hT_lo[:, k, tok], k == 0, k == KT - 1)
                mm.then_inc(al_ready, 1)
            pe.wait_ge(al_taken, 2)
            pe.wait_ge(small_landed, SMALL)
            for n in range(2 * GH):
                h, half = n // 2, n % 2
                if n >= 4:
                    pe.wait_ge(z_abs, n - 3)
                    pe.wait_ge(z_min, n - 3)
                nc.tensor.matmul(prog.ps[:, 4 + n % 4, :], wau[:, h * DK:(h + 1) * DK],
                                 AL[:, half * 512:(half + 1) * 512], start=True, stop=True).then_inc(z_ready, 1)
            for u in range(ROWS):
                pe_rows_unit(prog, pe, w, u, w.slot(u), acc_free, acc_ready, u * TT if u else None,
                             prog.hT_hi, prog.hT_lo)
            for u in range(ROWS, NU):
                base = TT * ROWS + 4 * (u - ROWS)
                pe_columns_unit(prog, pe, w, u, w.slot(u), lambda i, base=base: pe.wait_ge(acc_free, base + i - 3),
                                acc_ready, 0)

        @block.scalar
        def _(act):
            def take_v(u):
                for t in range(TT):
                    act.wait_ge(acc_ready, u * TT + t + 1)
                    nc.scalar.activation(V[:, t, u * UNIT:(u + 1) * UNIT], prog.ps[:, t % 4, 0:UNIT],
                                         ACT.Copy).then_inc(acc_free, 1)
                w.split_hi(act, u + 2)

            act.wait_ge(wa_landed, 16)
            nc.scalar.activation(wa_hi[:], wa_raw[:], ACT.Copy).then_inc(wa_split, 1)
            for half in range(2):
                act.wait_ge(al_ready, half + 1)
                nc.scalar.activation(AL[:, half * 512:(half + 1) * 512], prog.ps[0:RANK, 4 + half, :],
                                     ACT.Copy).then_inc(al_taken, 1)
            for n in range(2 * GH):
                h, half = n // 2, n % 2
                act.wait_ge(z_ready, n + 1)
                if n >= 2:
                    act.wait_ge(z_exp, n - 1)
                nc.scalar.activation(tmp[:, n % 2, :], prog.ps[:, 4 + n % 4, :], ACT.Abs,
                                     bias=ba[:, h:h + 1]).then_inc(z_abs, 1)
                act.wait_ge(z_abs, n + 1)
                nc.scalar.activation(B[:, h, half * 512:(half + 1) * 512], tmp[:, n % 2, :], ACT.Exp,
                                     scale=-1.0).then_inc(z_exp, 1)
            take_v(0)
            act.wait_ge(z_exp, 2 * GH)
            for h in range(GH):
                nc.scalar.activation(B[:, h, :], B[:, h, :], ACT.Ln, bias=1.0).then_inc(z_log, 1)
            take_v(1)
            for h in range(GH):
                act.wait_ge(b_done, h + 1)
                nc.scalar.activation(Q[:, h, :], B[:, h, :], ACT.Exp, scale=1.0 / TAU).then_inc(e_done, 1)
            nc.scalar.activation(DEC[:], Bv[:, :, :, CH - 1], ACT.Exp, scale=1.0 / TAU).then_inc(e_done, 1)
            take_v(2)
            act.wait_ge(e_done, GH + 1)
            for h in range(GH):
                nc.scalar.activation(B[:, h, :], B[:, h, :], ACT.Exp, scale=-1.0 / TAU).then_inc(e_done, 1)
            take_v(3)
            for u in range(ROWS, NU):
                w.split_hi(act, u + 2)

        @block.vector
        def _(dve):
            dve.wait_ge(small_landed, SMALL)
            dve.wait_ge(wa_split, 1)
            nc.vector.tensor_tensor(wa_lo[:], wa_raw[:], plane(wa_hi[:]), ALU.subtract).then_inc(wa_split, 1)
            for n in range(2 * GH):
                h, half = n // 2, n % 2
                dve.wait_ge(z_abs, n + 1)
                nc.vector.tensor_scalar(K[:, h, half * 512:(half + 1) * 512], prog.ps[:, 4 + n % 4, :],
                                        ba[:, h:h + 1], 0.0, ALU.add, ALU.min).then_inc(z_min, 1)
            w.split_lo(dve, 2)
            dve.wait_ge(keep_made, 2)
            for h in range(GH):
                dve.wait_ge(z_log, h + 1)
                dve.wait_ge(z_min, 2 * GH)
                nc.vector.tensor_tensor(K[:, h, :], K[:, h, :], B[:, h, :], ALU.subtract).then_inc(ls_done, 1)
                dve.wait_ge(ls_done, h + 1)
                nc.vector.tensor_tensor_scan(B[:, h, :], keep[:], K[:, h, :], 0.0, ALU.mult,
                                             ALU.add).then_inc(b_done, 1)
            for u in range(1, ROWS):
                w.split_lo(dve, u + 2)
            for u in range(ROWS, NU):
                for i in range(4):
                    h, half = (u % 2) * 2 + i // 2, i % 2
                    tok = slice(half * 512, (half + 1) * 512)
                    dve.wait_ge(acc_ready, TT * ROWS + 4 * (u - ROWS) + i + 1)
                    if u < ROWS + 2:
                        dve.wait_ge(e_done, GH + 1)
                        nc.vector.scalar_tensor_tensor(Q[:, h, tok], prog.ps[:, i, :], DK ** -0.5, Q[:, h, tok],
                                                       ALU.mult, ALU.mult).then_inc(acc_free, 1)
                    else:
                        dve.wait_ge(e_done, 2 * GH + 1)
                        nc.vector.tensor_tensor(K[:, h, tok], prog.ps[:, i, :], B[:, h, tok],
                                                ALU.mult).then_inc(acc_free, 1)
                w.split_lo(dve, u + 2)
    prog.end_phase()
    return Q, K, V, DEC


def gla_core(prog, a, Q, K, V, DEC, stream, follows):
    nc = prog.nc
    kb = prog.B
    NCH = SEQ // CH
    f = kb + 32
    S = prog.at("S", [P, 2, GH, P], f)
    KE = prog.at("KE", [P, 2, GH, P], f + 4)
    KEt = prog.at("KEt", [P, 2, GH, P], f + 8)
    stat = prog.at("stat", [P, 3, TT, GH], f + 12)
    gat = prog.at("gat", [P, 2, UNIT], f + 13)
    ST = prog.at("ST", [P, 2, GH, DV], kb + 80)
    mask = prog.at("mask", [P, P], f + 15, U32)
    on = prog.at("on", [P, GH * DV], kb + 88)
    junk = prog.at("junk", [P, DV], kb + 92.5)
    NU = 4

    acc_ready = prog.sem("acc_ready")
    w = Weights(prog, stream, NU, acc_ready, lambda u: (u + 1) * TT, follows)
    small_landed = prog.sem("small_landed")
    zeroed = prog.sem("zeroed")
    masked = prog.sem("masked")
    st_zero = prog.sem("st_zero")
    s_ready = prog.sem("s_ready")
    s_done = prog.sem("s_done")
    ke_done = prog.sem("ke_done")
    ke_turned = prog.sem("ke_turned")
    ke_taken = prog.sem("ke_taken")
    kv_ready = prog.sem("kv_ready")
    st_done = prog.sem("st_done")
    inter = prog.sem("inter")
    o_ready = prog.sem("o_ready")
    squared = prog.sem("squared")
    meaned = prog.sem("meaned")
    rooted = prog.sem("rooted")
    inverted = prog.sem("inverted")
    o_done = prog.sem("o_done")
    acc_free = prog.sem("acc_free")
    y_done = prog.sem("y_done")

    with nc.Block() as block:
        @block.sync
        def _(sp):
            sp.dma_start(on[:], a["gla_out_norm"].rearrange("(o n) -> o n", o=1).to_broadcast([P, GH * DV])
                         ).then_inc(small_landed, 16)
            for u in range(2, NU + 2):
                w.load(sp, u)

        @block.gpsimd
        def _(pool):
            nc.gpsimd.memset(mask[:].bitcast(F32), 1.0).then_inc(zeroed, 1)
            nc.gpsimd.memset(S[:], 0.0).then_inc(zeroed, 1)
            pool.wait_ge(zeroed, 2)
            nc.gpsimd.affine_select(out=mask[:].bitcast(F32), in_=mask[:].bitcast(F32), compare_op=ALU.is_ge,
                                    fill=0.0, base=0, pattern=[[1, P]], channel_multiplier=-1).then_inc(masked, 1)
            pool.wait_ge(masked, 1)
            nc.gpsimd.memset(mask[0:CH, CH:P].bitcast(F32), 0.0).then_inc(masked, 1)
            for t in range(TT):
                if t >= 2:
                    pool.wait_ge(ke_turned, t - 1)
                out = KE[:, t % 2, :, :].rearrange("p h (c s) -> p h c s", s=CH)
                k_in = K[:, :, t * P:(t + 1) * P].rearrange("p h (c s) -> p h c s", s=CH)
                for c in range(2):
                    ins = nc.gpsimd.tensor_tensor(out[:, :, c, :], k_in[:, :, c, :],
                                                  DEC[:, :, 2 * t + c].unsqueeze(2).to_broadcast([P, GH, CH]),
                                                  ALU.mult)
                    ins.then_inc(ke_done, 1)

        @block.tensor
        def _(pe):
            def tile_scores(t):
                if t >= 1:
                    pe.wait_ge(s_done, t)
                for h in range(GH):
                    mm = nc.tensor.matmul(prog.ps[:, 0, h * P:(h + 1) * P], K[:, h, t * P:(t + 1) * P],
                                          Q[:, h, t * P:(t + 1) * P], start=(h == 0), stop=True,
                                          skip_group_check=True)
                mm.then_inc(s_ready, 1)
                pe.wait_ge(ke_done, 2 * t + 2)
                if t >= 1:
                    pe.wait_ge(ke_taken, t)
                for h in range(GH):
                    mm = nc.tensor.transpose(prog.ps[:, 1, h * P:(h + 1) * P], KE[:, t % 2, h, :], prog.ident[:])
                mm.then_inc(ke_turned, 1)

            def keys_values(t, c):
                n = 2 * t + c
                if n >= 1:
                    pe.wait_ge(st_done, GH * n)
                rows = slice(c * CH, (c + 1) * CH)
                for h in range(GH):
                    mm = nc.tensor.matmul(prog.ps[:, 2 + h // 2, h % 2 * DV:(h % 2 + 1) * DV], KEt[rows, t % 2, h, :],
                                          V[rows, t, h * DV:(h + 1) * DV], start=(h % 2 == 0), stop=True,
                                          skip_group_check=True)
                mm.then_inc(kv_ready, 1)

            def outs(t, h):
                return prog.ps[:, 4 + 2 * (t % 2) + h // 2, h % 2 * DV:(h % 2 + 1) * DV]

            def within(t):
                pe.wait_ge(s_done, t + 1)
                if t >= 2:
                    pe.wait_ge(o_done, GH * (t - 1))
                for h in range(GH):
                    nc.tensor.matmul(outs(t, h), S[:, t % 2, h, :], V[:, t, h * DV:(h + 1) * DV],
                                     start=(h % 2 == 0), stop=False, skip_group_check=True)

            def from_state(t, c):
                n = 2 * t + c
                if n:
                    pe.wait_ge(st_done, GH * n)
                for h in range(GH):
                    cols = slice(t * P + c * CH, t * P + (c + 1) * CH)
                    mm = nc.tensor.matmul(outs(t, h)[c * CH:(c + 1) * CH], Q[:, h, cols], ST[:, n % 2, h, :],
                                          start=False, stop=True, skip_group_check=True)
                mm.then_inc(inter, 1)

            pe.wait_ge(st_zero, 1)
            tile_scores(0)
            for t in range(TT):
                pe.wait_ge(ke_taken, t + 1)
                keys_values(t, 0)
                within(t)
                from_state(t, 0)
                if t + 1 < TT:
                    tile_scores(t + 1)
                keys_values(t, 1)
                from_state(t, 1)
            pe.wait_ge(st_done, GH * NCH)
            for u in range(NU):
                pe_rows_unit(prog, pe, w, u, w.slot(u), acc_free, acc_ready, u * TT if u else None,
                             prog.hT_hi, prog.hT_lo)

        @block.scalar
        def _(act):
            def head_squares(t):
                act.wait_ge(inter, 2 * t + 2)
                for h in range(GH):
                    n = t * GH + h
                    if n:
                        act.wait_ge(squared, n)
                    nc.scalar.activation(junk[:], prog.ps[:, 4 + 2 * (t % 2) + h // 2, h % 2 * DV:(h % 2 + 1) * DV],
                                         ACT.Square, accum_out=stat[:, 0, t, h:h + 1]).then_inc(squared, 1)
                act.wait_ge(meaned, t + 1)
                nc.scalar.activation(stat[:, 2, t, :], stat[:, 1, t, :], ACT.Sqrt).then_inc(rooted, 1)

            for t in range(TT):
                act.wait_ge(ke_turned, t + 1)
                if t >= 2:
                    act.wait_ge(kv_ready, 2 * t - 2)
                nc.scalar.activation(KEt[:, t % 2, :, :], prog.ps[:, 1, :].rearrange("p (h d) -> p h d", h=GH),
                                     ACT.Copy).then_inc(ke_taken, 1)
                if t >= 1:
                    head_squares(t - 1)
            head_squares(TT - 1)
            for u in range(NU):
                for t in range(TT):
                    n = u * TT + t
                    act.wait_ge(acc_ready, n + 1)
                    if n >= 2:
                        act.wait_ge(y_done, n - 1)
                    nc.scalar.activation(gat[:, n % 2, :], prog.ps[:, t % 4, 0:UNIT], ACT.Silu).then_inc(acc_free, 1)
                w.split_hi(act, u + 2)

        @block.vector
        def _(dve):
            nc.vector.memset(ST[:, 0, :, :], 0.0).then_inc(st_zero, 1)
            dve.wait_ge(st_zero, 1)
            dve.wait_ge(zeroed, 2)
            dve.wait_ge(masked, 2)
            dve.wait_ge(small_landed, 16)

            def mask_scores(t):
                dve.wait_ge(s_ready, t + 1)
                if t >= 2:
                    dve.wait_ge(inter, 2 * t - 3)
                nc.vector.copy_predicated(S[:, t % 2, :, :], mask[:].unsqueeze(1).to_broadcast([P, GH, P]),
                                          prog.ps[:, 0, :].rearrange("p (h d) -> p h d", h=GH)).then_inc(s_done, 1)

            def state(t, c):
                n = 2 * t + c
                dve.wait_ge(kv_ready, n + 1)
                if n:
                    dve.wait_ge(inter, n)
                    dve.wait_ge(st_done, GH * n)
                for h in range(GH):
                    nc.vector.scalar_tensor_tensor(ST[:, (n + 1) % 2, h, :], ST[:, n % 2, h, :], DEC[:, h, n:n + 1],
                                                   prog.ps[:, 2 + h // 2, h % 2 * DV:(h % 2 + 1) * DV], ALU.mult,
                                                   ALU.add).then_inc(st_done, 1)

            def normed(t):
                dve.wait_ge(squared, GH * (t + 1))
                nc.vector.tensor_scalar(stat[:, 1, t, :], stat[:, 0, t, :], 1.0 / DV, EPS, ALU.mult,
                                        ALU.add).then_inc(meaned, 1)
                dve.wait_ge(rooted, t + 1)
                nc.vector.reciprocal(stat[:, 0, t, :], stat[:, 2, t, :]).then_inc(inverted, 1)
                dve.wait_ge(inverted, t + 1)
                for h in range(GH):
                    cols = slice(h * DV, (h + 1) * DV)
                    nc.vector.scalar_tensor_tensor(V[:, t, cols],
                                                   prog.ps[:, 4 + 2 * (t % 2) + h // 2, h % 2 * DV:(h % 2 + 1) * DV],
                                                   stat[:, 0, t, h:h + 1], on[:, cols], ALU.mult,
                                                   ALU.mult).then_inc(o_done, 1)

            mask_scores(0)
            for t in range(TT):
                state(t, 0)
                if t + 1 < TT:
                    mask_scores(t + 1)
                state(t, 1)
                if t >= 1:
                    normed(t - 1)
            normed(TT - 1)
            for u in range(NU):
                for t in range(TT):
                    n = u * TT + t
                    cols = slice(u * UNIT, (u + 1) * UNIT)
                    dve.wait_ge(acc_free, n + 1)
                    if n == 0:
                        dve.wait_ge(o_done, GH * TT)
                    nc.vector.tensor_tensor(V[:, t, cols], V[:, t, cols], gat[:, n % 2, :], ALU.mult).then_inc(y_done, 1)
                w.split_lo(dve, u + 2)
    prog.end_phase()


def up_stream(w_up):
    wv = w_up.rearrange("(k p) n -> p k n", p=P)

    def src(u, raw):
        raw = raw.rearrange("p (k n) -> p k n", k=KT)
        return [(raw[:, :, 0:P], wv[:, :, bass.ds(u * P, P)]),
                (raw[:, :, P:], wv[:, :, bass.ds(u * P + FFN, P)])]

    return Stream(src, pieces=2)


def ffn_up(prog, a, stream, follows):
    nc = prog.nc
    kb = prog.B
    A = prog.at("A", [P, FT, SEQ], kb)
    craw = prog.at("craw", [2 * FT, 4, P], kb + 48)
    CW = prog.at("CW", [P, 4, 2 * FT], kb + 92)
    CG = prog.at("CG", [P, SEQ], kb + 88)
    NU = FT

    acc_ready = prog.sem("acc_ready")
    w = Weights(prog, stream, NU, acc_ready, lambda u: u * 4 + 4, follows)
    small_landed = prog.sem("small_landed")
    cw_turned = prog.sem("cw_turned")
    cw_taken = prog.sem("cw_taken")
    newest_tap = prog.sem("newest_tap")
    tap = prog.sem("tap")
    gate_done = prog.sem("gate_done")
    a_done = prog.sem("a_done")

    with nc.Block() as block:
        @block.sync
        def _(sp):
            sp.dma_start(craw[:, 0:3, :], a["ffn_conv_w"].rearrange("j (f p) -> f j p", p=P)).then_inc(small_landed, 16)
            sp.dma_start(craw[:, 3, :], a["ffn_conv_b"].rearrange("(f p) -> f p", p=P)).then_inc(small_landed, 16)
            w.load(sp, 2)
            w.load(sp, 3)
            with sp.Fori(2, NU // 2) as pair:
                for j in range(2):
                    w.load(sp, pair * 2 + j, w.slot(j))
            w.load(sp, NU)
            w.load(sp, NU + 1)

        SMALL = 2 * 16

        @block.tensor
        def _(pe):
            pe_columns_unit(prog, pe, w, 0, w.slot(0), None, acc_ready, 0)
            pe.wait_ge(small_landed, SMALL)
            for j in range(4):
                mm = nc.tensor.transpose(prog.ps[:, 4, j * 2 * FT:(j + 1) * 2 * FT], craw[:, j, :],
                                         prog.ident[0:2 * FT, 0:2 * FT])
            mm.then_inc(cw_turned, 1)
            pe.wait_ge(cw_taken, 1)
            pe_columns_unit(prog, pe, w, 1, w.slot(1), None, acc_ready, 4)
            with pe.Fori(1, NU // 2) as pair:
                for j in range(2):
                    u = pair * 2 + j
                    pe.wait_ge(tap, u * 4 - 4)
                    pe_columns_unit(prog, pe, w, u, w.slot(j), None, acc_ready, 4 * j)

        def banks(j, part):
            return prog.ps[:, 4 * j + 2 * part:4 * j + 2 * part + 2, :].rearrange("p a b -> p (a b)")

        @block.scalar
        def _(act):
            act.wait_ge(cw_turned, 1)
            nc.scalar.activation(CW[:].rearrange("p j f -> p (j f)"), prog.ps[:, 4, 0:8 * FT],
                                 ACT.Copy).then_inc(cw_taken, 1)
            act.wait_ge(cw_taken, 1)

            def unit(u, j, first=False, pair=None):
                if not first:
                    act.wait_ge(a_done, u)
                act.wait_ge(acc_ready, u * 4 + 2)
                nc.scalar.activation(CG[:], banks(j, 0), ACT.Identity, bias=CW[:, 3, bass.ds(u, 1)],
                                     scale=CW[:, 2, bass.ds(u, 1)]).then_inc(newest_tap, 1)
                act.wait_ge(acc_ready, u * 4 + 4)
                nc.scalar.activation(A[:, bass.ds(u, 1), :], banks(j, 1), ACT.Identity,
                                     bias=CW[:, 3, bass.ds(u + FT, 1)],
                                     scale=CW[:, 2, bass.ds(u + FT, 1)]).then_inc(newest_tap, 1)
                if pair is None:
                    w.split_hi(act, u + 2)
                else:
                    w.split_hi(act, u + 2, w.slot(j), pair + 1)
                act.wait_ge(tap, u * 4 + 2)
                nc.scalar.activation(CG[:], CG[:], ACT.Silu).then_inc(gate_done, 1)

            unit(0, 0, first=True)
            unit(1, 1)
            with act.Fori(1, NU // 2 - 1) as pair:
                for j in range(2):
                    unit(pair * 2 + j, j, pair=pair)
            for u in (NU - 2, NU - 1):
                unit(u, u % 2)

        @block.vector
        def _(dve):
            dve.wait_ge(cw_taken, 1)

            def unit(u, j):
                for part, (dst, f) in enumerate(((CG[:].unsqueeze(1), u), (A[:, bass.ds(u, 1), :], u + FT))):
                    dve.wait_ge(newest_tap, u * 2 + part + 1)
                    for back in (1, 2):
                        out = dst[:, :, back:]
                        nc.vector.scalar_tensor_tensor(out, banks(j, part)[:, 0:SEQ - back].unsqueeze(1),
                                                       CW[:, 2 - back, bass.ds(f, 1)], out, ALU.mult,
                                                       ALU.add).then_inc(tap, 1)
                        dve.wait_ge(tap, u * 4 + 2 * part + back)
                w.split_lo(dve, u + 2, w.slot(j))
                dve.wait_ge(gate_done, u + 1)
                nc.vector.tensor_tensor(A[:, bass.ds(u, 1), :], A[:, bass.ds(u, 1), :], CG[:].unsqueeze(1),
                                        ALU.mult).then_inc(a_done, 1)

            with dve.Fori(0, NU // 2 - 1) as pair:
                for j in range(2):
                    unit(pair * 2 + j, j)
            for u in (NU - 2, NU - 1):
                unit(u, u % 2)
    prog.end_phase()
    return A


DOWN_KU = 2
DOWN_COLS = 512


def down_stream(w_down):
    wv = w_down.rearrange("(k p) n -> p k n", p=P)
    NU = FT // DOWN_KU

    def src(u, raw):
        k0, half = u % NU * DOWN_KU, u // NU
        return [(raw.rearrange("p (k n) -> p k n", k=DOWN_KU),
                 wv[:, k0:k0 + DOWN_KU, half * DOWN_COLS:(half + 1) * DOWN_COLS])]

    return Stream(src, size=DOWN_KU * DOWN_COLS)


def ffn_down(prog, a, A, x_src, out, stream):
    nc = prog.nc
    kb = prog.B
    KU, NCOL = DOWN_KU, DOWN_COLS
    NU = FT // KU
    A_hi = prog.at("A_hi", [P, 2, KU, SEQ], 0, F32R)
    A_lo = prog.at("A_lo", [P, 2, KU, SEQ], 16, F32R)
    O = prog.at("O", [P, TT, D], 32)
    fg = prog.at("fg", [P, D], 84)
    junk = prog.at("junk", [P, NCOL], 92)
    stat = prog.at("stat", [P, 40], kb + 93)
    done = prog.sem("unit_done")

    w = Weights(prog, stream, 2 * NU, done, None, None)
    a_hi = prog.sem("a_hi_ready")
    a_lo = prog.sem("a_lo_ready")
    out_ready = prog.sem("out_ready")
    out_free = prog.sem("out_free")
    fg_landed = prog.sem("fg_landed")
    x_landed = prog.sem("x_landed")
    squared = prog.sem("squared")
    summed = prog.sem("summed")
    rooted = prog.sem("rooted")
    inverted = prog.sem("inverted")
    scaled = prog.sem("scaled")
    y_even = prog.sem("y_done_even")
    y_odd = prog.sem("y_done_odd")
    stored = prog.sem("stored")
    xv = x_src.rearrange("(t p) d -> p t d", p=P)
    ov = out.rearrange("(t p) d -> p t d", p=P)

    def tiles(u):
        i = u % NU
        return A[:, KU * i:KU * (i + 1), :]

    with nc.Block() as block:
        @block.sync
        def _(sp):
            w.load(sp, 2)
            w.load(sp, 3)
            sp.dma_start(fg[:], a["final_norm"].rearrange("(o n) -> o n", o=1).to_broadcast([P, D])
                         ).then_inc(fg_landed, 16)
            for u in range(4, 2 * NU):
                w.load(sp, u)
                if u - 4 < TT:
                    sp.dma_start(O[:, u - 4, :], xv[:, u - 4, :]).then_inc(x_landed, 16)
            for t in range(TT):
                sp.wait_ge(y_even if t % 2 == 0 else y_odd, t // 2 + 1)
                sp.dma_start(ov[:, t, :], O[:, t, :]).then_inc(stored, 16)
            sp.wait_ge(stored, 16 * TT)

        @block.tensor
        def _(pe):
            def unit(u, slot, first=False, last=False, fresh=False):
                if not isinstance(u, int) or u >= 2:
                    w.ready(pe, u)
                pe.wait_ge(a_lo, u + 1)
                order = [(k, t) for k in range(KU) for t in range(TT)]
                if last:
                    order = [(k, t) for t in range(TT) for k in range(KU)]
                for k, t in order:
                    if first and k == 0 and not fresh:
                        pe.wait_ge(out_free, t + 1)
                    tok = slice(t * P, (t + 1) * P)
                    col = slice(k * NCOL, (k + 1) * NCOL)
                    mm = three_products(nc, prog.ps[:, t, :], A_hi[:, slot, k, tok], A_lo[:, slot, k, tok],
                                        prog.w_hi[:, slot, col], prog.w_lo[:, slot, col],
                                        first and k == 0, last and k == KU - 1)
                    if last and k == KU - 1:
                        mm.then_inc(out_ready, 1)
                    elif not last and k == KU - 1 and t == TT - 1:
                        mm.then_inc(done, 1)

            for half in range(2):
                u0 = half * NU
                unit(u0, u0 % 2, first=True, fresh=(half == 0))
                with pe.Fori(0, (NU - 3) // 2) as pair:
                    for j in range(2):
                        unit(pair * 2 + (u0 + 1 + j), (u0 + 1 + j) % 2)
                unit(u0 + NU - 2, (u0 + NU - 2) % 2)
                unit(u0 + NU - 1, (u0 + NU - 1) % 2, last=True)

        @block.scalar
        def _(act):
            def split(u):
                if u >= 2:
                    if u - 2 < NU - 1:
                        act.wait_ge(done, u - 1)
                    elif u - 2 == NU - 1:
                        act.wait_ge(out_ready, TT)
                    else:
                        act.wait_ge(done, u - 2)
                if u >= 2:
                    w.split_hi(act, u, wait_pe=False)
                nc.scalar.activation(A_hi[:, u % 2, :, :], tiles(u), ACT.Copy).then_inc(a_hi, 1)

            def square(half, t):
                act.wait_ge(out_free, half * TT + t + 1)
                if half or t:
                    act.wait_ge(squared, half * TT + t)
                nc.scalar.activation(junk[:], O[:, t, half * NCOL:(half + 1) * NCOL], ACT.Square,
                                     accum_out=stat[:, half * TT + t:half * TT + t + 1]).then_inc(squared, 1)

            for u in range(NU + 2):
                split(u)
            for t in range(TT):
                square(0, t)
            for u in range(NU + 2, 2 * NU):
                split(u)
            for g in range(TT // 2 + 1):
                if g < TT // 2:
                    square(1, 2 * g)
                    square(1, 2 * g + 1)
                if g >= 1:
                    act.wait_ge(summed, g)
                    nc.scalar.activation(stat[:, 22 + 2 * g:24 + 2 * g], stat[:, 14 + 2 * g:16 + 2 * g], ACT.Sqrt,
                                         bias=prog.eps[:], scale=1.0 / D).then_inc(rooted, 1)
                    t = 2 * g - 1
                    act.wait_ge(inverted, g)
                    nc.scalar.activation(O[:, t, :], O[:, t, :], ACT.Copy,
                                         scale=stat[:, 32 + t:33 + t]).then_inc(scaled, 1)

        @block.gpsimd
        def _(pool):
            pool.wait_ge(fg_landed, 16)
            for t in range(1, TT, 2):
                pool.wait_ge(scaled, t // 2 + 1)
                nc.gpsimd.tensor_tensor(O[:, t, :], O[:, t, :], fg[:], ALU.mult).then_inc(y_odd, 1)

        @block.vector
        def _(dve):
            def split(u):
                if u >= 2:
                    w.split_lo(dve, u)
                dve.wait_ge(a_hi, u + 1)
                nc.vector.tensor_tensor(A_lo[:, u % 2, :, :], tiles(u), plane(A_hi[:, u % 2, :, :]),
                                        ALU.subtract).then_inc(a_lo, 1)

            def take(half, t):
                dve.wait_ge(out_ready, half * TT + t + 1)
                cols = slice(half * NCOL, (half + 1) * NCOL)
                nc.vector.tensor_tensor(O[:, t, cols], prog.ps[:, t, :], O[:, t, cols], ALU.add).then_inc(out_free, 1)

            for u in range(NU + 1):
                split(u)
            dve.wait_ge(x_landed, 16 * TT)
            for t in range(TT):
                take(0, t)
            for u in range(NU + 1, 2 * NU):
                split(u)
            dve.wait_ge(fg_landed, 16)
            for g in range(TT // 2 + 1):
                if g < TT // 2:
                    take(1, 2 * g)
                    take(1, 2 * g + 1)
                if g >= 1:
                    t = 2 * g - 2
                    dve.wait_ge(squared, TT + 2 * g)
                    nc.vector.tensor_tensor(stat[:, 16 + t:18 + t], stat[:, t:t + 2], stat[:, 8 + t:10 + t],
                                            ALU.add).then_inc(summed, 1)
                    dve.wait_ge(rooted, g)
                    nc.vector.reciprocal(stat[:, 32 + t:34 + t], stat[:, 24 + t:26 + t]).then_inc(inverted, 1)
                    dve.wait_ge(inverted, g)
                    nc.vector.scalar_tensor_tensor(O[:, t, :], O[:, t, :], stat[:, 32 + t:33 + t], fg[:], ALU.mult,
                                                   ALU.mult).then_inc(y_even, 1)
    prog.end_phase()


def build(nc, a, out):
    with ExitStack() as ctx:
        prog = Program(nc, ctx, a)
        x_mid = nc.dram_tensor("x_mid", (SEQ, D), F32).ap()
        ins = [column_stream(a["w_in"][l], MIXER_ORDER) for l in range(DEPTH)]
        outs = [column_stream(a["w_out"][l], [u * UNIT for u in range(4)]) for l in range(DEPTH)]
        gla_in = column_stream(a["gla_w_in"], GLA_ORDER)
        gla_r = column_stream(a["gla_w_in"], [2048 + u * UNIT for u in range(4)])
        gla_out = column_stream(a["gla_w_out"], [u * UNIT for u in range(4)])
        up, down = up_stream(a["ffn_w_up"]), down_stream(a["ffn_w_down"])

        def row(v):
            return v.rearrange("(o n) -> o n", o=1)

        start(prog, a, ins[0], a["pre_g"][0:1, :])
        for l in range(DEPTH):
            last = l == DEPTH - 1
            QKV, U, G = mixer_inputs(prog, l, a, ins[l], outs[l])
            attention(prog, l, QKV, G)

            def rows(t, k):
                src, k = (U, k) if k < 4 else (G, k - 4)
                return src[:, t, k * P:(k + 1) * P]

            output_rows(prog, outs[l], gla_in if last else ins[l + 1], a["post_g"][l:l + 1, :],
                        row(a["norm1"]) if last else a["pre_g"][l + 1:l + 2, :], rows,
                        a["x"][0] if l == 0 else x_mid, x_mid)
        Q, K, V, DEC = gla_inputs(prog, a, gla_in, gla_r)
        gla_core(prog, a, Q, K, V, DEC, gla_r, gla_out)
        output_rows(prog, gla_out, up, None, row(a["norm2"]), lambda t, k: V[:, t, k * P:(k + 1) * P], x_mid, x_mid)
        A = ffn_up(prog, a, up, down)
        ffn_down(prog, a, A, x_mid, out[0], down)


_USED = ["x", "w_in", "w_out", "pre_g", "post_g", "ln_a_g", "ln_a_b", "spatial_w", "spatial_b", "q_norm_g",
         "k_norm_g"]
_SECOND = ["norm1", "gla_w_in", "gla_w_alpha_up", "gla_b_alpha", "gla_out_norm", "gla_w_out", "norm2", "ffn_w_up",
           "ffn_conv_w", "ffn_conv_b", "ffn_w_down"]


def rope_tables():
    import numpy as np
    pos = np.arange(SEQ)
    row, col = (pos // 64).astype(np.float32), (pos % 64).astype(np.float32)
    inv = (np.float32(10000.0) ** (-np.arange(0, 32, 2, dtype=np.float32) / np.float32(32))).astype(np.float32)
    ar, ac = row[:, None] * inv, col[:, None] * inv
    cos = np.concatenate([np.cos(ar), np.cos(ar), np.cos(ac), np.cos(ac)], 1)
    sin = np.concatenate([-np.sin(ar), np.sin(ar), -np.sin(ac), np.sin(ac)], 1)
    return np.stack([cos, sin]).astype(np.float32)


def kernel(**inputs):
    import numpy as np
    import concourse.bacc as bacc
    from concourse import mybir as mb
    from concourse.bass_utils import run_bass_kernel_spmd as run

    nc = bacc.Bacc("TRN2", target_bir_lowering=False, num_devices=1)
    arrays, args = {}, {}
    given = {n: np.ascontiguousarray(inputs[n]) for n in _USED}
    given.update({n: np.ascontiguousarray(inputs[f"l0_{n}_2"]) for n in _SECOND})
    given["final_norm"] = np.ascontiguousarray(inputs["final_norm_2"])
    given["rope"] = rope_tables()
    for name, v in given.items():
        arrays[f"in_{name}"] = v
        args[name] = nc.dram_tensor(f"in_{name}", v.shape, mb.dt.from_np(v.dtype), kind="ExternalInput").ap()
    out = nc.dram_tensor("out", (1, SEQ, D), mb.dt.float32, kind="ExternalOutput").ap()
    build(nc, args, out)
    r = run(nc, [arrays], core_ids=[0])
    return r.results[0]["out"]
```
